# Optimizing a Trainium2 kernel written in Bass

```python
import jax
import jax.numpy as jnp
from jax import lax
import numpy as np

D_MODEL = 1024
BATCH = 1
SEQ = 256
DEPTH = 2

GRID_W = 64
CTX_LEN = 256
HEAD_DIM = 64
NA_HEADS = D_MODEL // (2 * HEAD_DIM)
GQA_HEADS = D_MODEL // (2 * HEAD_DIM)
GQA_KV_HEADS = GQA_HEADS // 4
GQA_GROUP = GQA_HEADS // GQA_KV_HEADS
NA_WIDTH = NA_HEADS * HEAD_DIM
GQA_WIDTH = GQA_HEADS * HEAD_DIM
GQA_KV_WIDTH = GQA_KV_HEADS * HEAD_DIM
MIX_WIDTH = NA_WIDTH + GQA_WIDTH
IN_WIDTH = 3 * NA_WIDTH + GQA_WIDTH + 2 * GQA_KV_WIDTH
IN_SPLITS = (NA_WIDTH, 2 * NA_WIDTH, 3 * NA_WIDTH, 3 * NA_WIDTH + GQA_WIDTH,
             3 * NA_WIDTH + GQA_WIDTH + GQA_KV_WIDTH)
NA_WIN_H = 8
NA_WIN_W = 16
RPB_H = 2 * NA_WIN_H - 1
RPB_W = 2 * NA_WIN_W - 1
D_FF = 2816
N_MOD = 9
Q_BLOCK = 128
ROPE_THETA = 10000.0
EPS = 1e-6
NEG_INF = -1e30

kernel_name = 'hybrid_na_gqa_macaron_dit'

def rms_norm(x, g):
    xf = x.astype(jnp.float32)
    y = xf * lax.rsqrt(jnp.mean(xf * xf, axis=-1, keepdims=True) + EPS)
    return (y * g.astype(jnp.float32)).astype(x.dtype)

def modulate(h, shift, scale):
    return h * (1 + scale) + shift

def ada_mod(cond, w_mod, b_mod):
    m = (jax.nn.silu(cond) @ w_mod + b_mod)[..., None, :]
    return jnp.split(m, N_MOD, axis=-1)

def swiglu(h, w13, w2):
    a, g = jnp.split(h @ w13, 2, axis=-1)
    return (jax.nn.silu(g) * a) @ w2

def ffn_half(x, norm_g, shift, scale, gate, w13, w2):
    h = modulate(rms_norm(x, norm_g), shift, scale)
    return x + 0.5 * gate * swiglu(h, w13, w2)

def axial_rope_tables(seq_len, dtype):
    t = jnp.arange(seq_len, dtype=jnp.int32)
    row = (t // GRID_W).astype(jnp.float32)
    col = (t % GRID_W).astype(jnp.float32)
    axis_dim = HEAD_DIM // 2
    inv_freq = ROPE_THETA ** (-jnp.arange(0, axis_dim, 2, dtype=jnp.float32) / axis_dim)
    ang_r = row[:, None] * inv_freq[None, :]
    ang_c = col[:, None] * inv_freq[None, :]
    return (jnp.cos(ang_r).astype(dtype), jnp.sin(ang_r).astype(dtype),
            jnp.cos(ang_c).astype(dtype), jnp.sin(ang_c).astype(dtype))

def rope_1d(x, cos, sin):
    x1, x2 = jnp.split(x, 2, axis=-1)
    return jnp.concatenate([x1 * cos - x2 * sin, x2 * cos + x1 * sin], axis=-1)

def apply_axial_rope(x, rope):
    cos_r, sin_r, cos_c, sin_c = rope
    xr, xc = jnp.split(x, 2, axis=-1)
    return jnp.concatenate([rope_1d(xr, cos_r, sin_r), rope_1d(xc, cos_c, sin_c)], axis=-1)

def split_heads(t, n_heads):
    b, l, _ = t.shape
    return t.reshape(b, l, n_heads, HEAD_DIM).transpose(0, 2, 1, 3)

def merge_heads(t):
    b, h, l, d = t.shape
    return t.transpose(0, 2, 1, 3).reshape(b, l, h * d)

def combined_projection(h, w_in):
    qa, ka, va, qb, kb, vb = jnp.split(h @ w_in, IN_SPLITS, axis=-1)
    return (split_heads(qa, NA_HEADS), split_heads(ka, NA_HEADS), split_heads(va, NA_HEADS),
            split_heads(qb, GQA_HEADS), split_heads(kb, GQA_KV_HEADS), split_heads(vb, GQA_KV_HEADS))

def neighbourhood_attention(q, k, v, k_ctx, v_ctx, rpb):
    b, h, l, d = q.shape
    rows = l // GRID_W
    kh = min(NA_WIN_H, rows)
    scale = d ** -0.5
    qg = q.reshape(b, h, rows, GRID_W, d)
    kg = k.reshape(b, h, rows, GRID_W, d)
    vg = v.reshape(b, h, rows, GRID_W, d)
    r = jnp.arange(rows)
    row_start = jnp.clip(r - kh // 2, 0, rows - kh)
    key_rows = row_start[:, None] + jnp.arange(kh)[None, :]
    k_blk = kg[:, :, key_rows]
    v_blk = vg[:, :, key_rows]
    cq = jnp.arange(GRID_W)
    col_start = jnp.clip(cq - NA_WIN_W // 2, 0, GRID_W - NA_WIN_W)
    in_win = (cq[None, :] >= col_start[:, None]) & (cq[None, :] < col_start[:, None] + NA_WIN_W)
    row_off = key_rows - r[:, None]
    col_off = jnp.clip(cq[None, :] - cq[:, None] + NA_WIN_W - 1, 0, RPB_W - 1)
    bias = rpb[:, (row_off + NA_WIN_H - 1)[:, None, :, None], col_off[None, :, None, :]]
    s_loc = jnp.einsum('bhrqd,bhrnkd->bhrqnk', qg, k_blk).astype(jnp.float32) * scale
    s_loc = s_loc + bias[None].astype(jnp.float32)
    s_loc = jnp.where(in_win[:, None, :], s_loc, NEG_INF)
    s_loc = s_loc.reshape(b, h, rows, GRID_W, kh * GRID_W)
    s_ctx = jnp.einsum('bhrqd,bhcd->bhrqc', qg, k_ctx).astype(jnp.float32) * scale
    p = jax.nn.softmax(jnp.concatenate([s_loc, s_ctx], axis=-1), axis=-1).astype(v.dtype)
    p_loc = p[..., :kh * GRID_W].reshape(b, h, rows, GRID_W, kh, GRID_W)
    p_ctx = p[..., kh * GRID_W:]
    o = (jnp.einsum('bhrqnk,bhrnkd->bhrqd', p_loc, v_blk)
         + jnp.einsum('bhrqc,bhcd->bhrqd', p_ctx, v_ctx))
    return o.reshape(b, h, l, d)

def gqa_blocked_attention(q, k_all, v_all):
    b, kvh, g, l, d = q.shape
    scale = d ** -0.5
    nb = l // Q_BLOCK
    qb = q.reshape(b, kvh, g, nb, Q_BLOCK, d).transpose(3, 0, 1, 2, 4, 5)

    def one_block(q_blk):
        s = jnp.einsum('bkgqd,bknd->bkgqn', q_blk, k_all).astype(jnp.float32) * scale
        p = jax.nn.softmax(s, axis=-1).astype(v_all.dtype)
        return jnp.einsum('bkgqn,bknd->bkgqd', p, v_all)

    o = lax.map(one_block, qb)
    return o.transpose(1, 2, 3, 0, 4, 5).reshape(b, kvh, g, l, d)

def dense_group_attention(q, k, v):
    s = jnp.einsum('bkgqd,bkcd->bkgqc', q, k).astype(jnp.float32) * (q.shape[-1] ** -0.5)
    p = jax.nn.softmax(s, axis=-1).astype(v.dtype)
    return jnp.einsum('bkgqc,bkcd->bkgqd', p, v)

def merge_groups(o_a, o_b, g_a, g_b, w_out):
    y = jnp.concatenate([rms_norm(merge_heads(o_a), g_a), rms_norm(merge_heads(o_b), g_b)], axis=-1)
    return y @ w_out

def mixer_sublayer(x, x_ctx, mod, mod_ctx, norm_g, w_in, rpb, q_norm, k_norm, g_a, g_b, w_out, rope, update_ctx):
    shift, scale, gate = mod
    shift_c, scale_c, gate_c = mod_ctx
    h = modulate(rms_norm(x, norm_g), shift, scale)
    h_c = modulate(rms_norm(x_ctx, norm_g), shift_c, scale_c)
    qa, ka, va, qb, kb, vb = combined_projection(h, w_in)
    qa_c, ka_c, va_c, qb_c, kb_c, vb_c = combined_projection(h_c, w_in)
    kb_c = rms_norm(kb_c, k_norm)
    o_a = neighbourhood_attention(qa, ka, va, ka_c, va_c, rpb)
    qb = apply_axial_rope(rms_norm(qb, q_norm), rope)
    kb = apply_axial_rope(rms_norm(kb, k_norm), rope)
    b, _, l, _ = qb.shape
    k_all = jnp.concatenate([kb, kb_c], axis=2)
    v_all = jnp.concatenate([vb, vb_c], axis=2)
    o_b = gqa_blocked_attention(qb.reshape(b, GQA_KV_HEADS, GQA_GROUP, l, HEAD_DIM), k_all, v_all)
    o_b = o_b.reshape(b, GQA_HEADS, l, HEAD_DIM)
    x = x + gate * merge_groups(o_a, o_b, g_a, g_b, w_out)
    if update_ctx:
        cl = x_ctx.shape[1]
        o_a_c = dense_group_attention(qa_c[:, :, None], ka_c, va_c)[:, :, 0]
        o_b_c = dense_group_attention(
            rms_norm(qb_c, q_norm).reshape(b, GQA_KV_HEADS, GQA_GROUP, cl, HEAD_DIM), kb_c, vb_c)
        o_b_c = o_b_c.reshape(b, GQA_HEADS, cl, HEAD_DIM)
        x_ctx = x_ctx + gate_c * merge_groups(o_a_c, o_b_c, g_a, g_b, w_out)
    return x, x_ctx

def setup_inputs(seed: int = 0) -> dict:
    key = jax.random.key(seed)
    ks = jax.random.split(key, 24)
    f32 = jnp.float32

    def nrm(k, shape, s):
        return jax.random.normal(k, shape, f32) * s

    def gain(k, shape):
        return 1.0 + 0.05 * jax.random.normal(k, shape, f32)

    return {
        'x': nrm(ks[0], (BATCH, SEQ, D_MODEL), 1.0),
        'c': nrm(ks[1], (BATCH, D_MODEL), 1.0),
        'ctx': nrm(ks[2], (BATCH, CTX_LEN, D_MODEL), 1.0),
        'c_ctx': nrm(ks[3], (D_MODEL,), 1.0),
        'w_mod': nrm(ks[4], (DEPTH, D_MODEL, N_MOD * D_MODEL), 0.5 * D_MODEL ** -0.5),
        'b_mod': nrm(ks[5], (DEPTH, N_MOD * D_MODEL), 0.01),
        'norm_ffn1': gain(ks[6], (DEPTH, D_MODEL)),
        'ffn1_w13': nrm(ks[7], (DEPTH, D_MODEL, 2 * D_FF), D_MODEL ** -0.5),
        'ffn1_w2': nrm(ks[8], (DEPTH, D_FF, D_MODEL), D_FF ** -0.5),
        'norm_mix': gain(ks[9], (DEPTH, D_MODEL)),
        'w_in': nrm(ks[10], (DEPTH, D_MODEL, IN_WIDTH), D_MODEL ** -0.5),
        'na_rpb': nrm(ks[11], (DEPTH, NA_HEADS, RPB_H, RPB_W), 0.1),
        'gqa_q_norm': gain(ks[12], (DEPTH, HEAD_DIM)),
        'gqa_k_norm': gain(ks[13], (DEPTH, HEAD_DIM)),
        'out_norm_a': gain(ks[14], (DEPTH, NA_WIDTH)),
        'out_norm_b': gain(ks[15], (DEPTH, GQA_WIDTH)),
        'w_out': nrm(ks[16], (DEPTH, MIX_WIDTH, D_MODEL), MIX_WIDTH ** -0.5),
        'norm_ffn2': gain(ks[17], (DEPTH, D_MODEL)),
        'ffn2_w13': nrm(ks[18], (DEPTH, D_MODEL, 2 * D_FF), D_MODEL ** -0.5),
        'ffn2_w2': nrm(ks[19], (DEPTH, D_FF, D_MODEL), D_FF ** -0.5),
        'norm_f': gain(ks[20], (D_MODEL,)),
    }

def reference(x, c, ctx, c_ctx, w_mod, b_mod, norm_ffn1, ffn1_w13, ffn1_w2, norm_mix, w_in, na_rpb,
              gqa_q_norm, gqa_k_norm, out_norm_a, out_norm_b, w_out, norm_ffn2, ffn2_w13, ffn2_w2, norm_f):
    rope = axial_rope_tables(x.shape[1], x.dtype)
    x_ctx = ctx
    for i in range(DEPTH):
        last = i == DEPTH - 1
        m = ada_mod(c, w_mod[i], b_mod[i])
        mc = ada_mod(c_ctx, w_mod[i], b_mod[i])
        x = ffn_half(x, norm_ffn1[i], m[0], m[1], m[2], ffn1_w13[i], ffn1_w2[i])
        x_ctx = ffn_half(x_ctx, norm_ffn1[i], mc[0], mc[1], mc[2], ffn1_w13[i], ffn1_w2[i])
        x, x_ctx = mixer_sublayer(x, x_ctx, m[3:6], mc[3:6], norm_mix[i], w_in[i], na_rpb[i],
                                  gqa_q_norm[i], gqa_k_norm[i], out_norm_a[i], out_norm_b[i], w_out[i],
                                  rope, not last)
        x = ffn_half(x, norm_ffn2[i], m[6], m[7], m[8], ffn2_w13[i], ffn2_w2[i])
        if not last:
            x_ctx = ffn_half(x_ctx, norm_ffn2[i], mc[6], mc[7], mc[8], ffn2_w13[i], ffn2_w2[i])
    return rms_norm(x, norm_f)


_drawn_inputs = setup_inputs


def setup_inputs(seed=0):
    import zlib

    import numpy as np

    out = dict(_drawn_inputs(seed))
    spreads = {}
    factors = {'norm_ffn1': 5.451,
     'norm_mix': 3.332,
     'na_rpb': 8.0,
     'gqa_q_norm': 8.0,
     'gqa_k_norm': 8.0,
     'out_norm_a': 3.628,
     'out_norm_b': 3.476,
     'norm_ffn2': 5.781}
    for name, (base, spread) in spreads.items():
        noise = np.random.default_rng([zlib.crc32(name.encode()), seed]).standard_normal(out[name].shape)
        drawn = base * np.exp(spread * noise) if base else spread * noise
        out[name] = jnp.asarray(drawn.astype(out[name].dtype))
    for name, factor in factors.items():
        out[name] = (out[name] * factor).astype(out[name].dtype)
    return out
```

```python
from contextlib import ExitStack

import numpy as np

import concourse.bass as bass
from concourse import mybir

F32 = mybir.dt.float32
F32R = mybir.dt.float32r
ACT = mybir.ActivationFunctionType
ALU = mybir.AluOpType

P = 128
D = 1024
KT = D // P
DEPTH = 2
LAT = 256
TOK = 512
HD = 64
HEADS = 8
GRID_W = 64
ROWS = LAT // GRID_W
WIN_W = 16
RPB_H, RPB_W = 15, 31
FF = 2816
N_MOD = 9
EPS = 1e-6
SCALE = HD ** -0.5
ROPE_THETA = 10000.0
UW = 256
IN_W = 2304
QB_COL = 1536

CHUNKS = (4, 4, 3)
W2_UNITS = D // UW
FFN_UNITS = 2 * sum(CHUNKS) + W2_UNITS * len(CHUNKS)
IN_UNITS = IN_W // UW
OUT_UNITS = D // UW
LAYER_UNITS = 2 * FFN_UNITS + IN_UNITS + OUT_UNITS
UNITS = DEPTH * LAYER_UNITS
HTILES = FF // P
X_PER_FFN = KT * len(CHUNKS)

MODS = DEPTH * N_MOD * D // UW
MODS_FIRST = 2 * D // UW
MODS_FFN = 2 * sum(CHUNKS)
MOD_ATT0 = MODS_FIRST + MODS_FFN

CHAINS = 5
PLAIN = 13

V_N1, V_NMIX, V_N2, V_GO, V_QN, V_KN, V_NF, V_C, V_COLS = 0, 8, 16, 24, 32, 33, 34, 42, 58
C_ID, C_BLK, C_ROT, C_COS, C_SIN, C_COLS = 0, 128, 256, 384, 640, 896

TOKENS2 = 2


def ffn_unit(layer, second):
    return layer * LAYER_UNITS + (FFN_UNITS + IN_UNITS + OUT_UNITS if second else 0)


def in_unit(layer):
    return layer * LAYER_UNITS + FFN_UNITS


def out_unit(layer):
    return in_unit(layer) + IN_UNITS


def x_before(layer, stage):
    return layer * (2 * X_PER_FFN + KT) + (0, X_PER_FFN, X_PER_FFN + KT)[stage]


def items(layer):
    tiles = range(4) if layer < DEPTH - 1 else range(2)
    return [(g, tt, h) for g in (True, False) for tt in tiles for h in range(HEADS)]


ITEMS0 = (0, len(items(0)), len(items(0)) + len(items(1)))


def build(nc, xT, ctxT, vecs, bmod, consts, w_mod, w13_1, w2_1, w_in, rpb, w_out, w13_2, w2_2, outT):
    ctx = ExitStack()
    with ctx:
        def sem(name):
            return ctx.enter_context(nc.semaphore(name))

        at = [16512]

        def place(name, shape, dt, where=None):
            size = -(-4 * int(np.prod(shape[1:])) // 32) * 32
            if where is None:
                where = at[0]
                at[0] += size
            return nc.alloc_sbuf_tensor_at(name, shape, dt, offset=where)

        x = place("x", [P, KT, TOK], F32)
        h_hi_at = at[0]
        h_hi = place("h_hi", [P, KT, TOK], F32R)
        h_lo_at = at[0]
        h_lo = place("h_lo", [P, KT, TOK], F32R)
        o = place("o", [P, 4, D], F32, h_hi_at)
        y_out = place("y_out", [P, KT, LAT], F32, h_hi_at)
        bias = place("bias", [P, 2, HEADS, ROWS, GRID_W], F32, h_lo_at)
        hid_hi = place("hid_hi", [P, 8, TOK], F32R)
        hid_lo = place("hid_lo", [P, 8, TOK], F32R)
        raw = [place(f"raw{s}", [P, KT, UW], F32) for s in range(2)]
        mraw = [place(f"mraw{s}", [P, KT, UW], F32) for s in range(2)]
        whi = [place(f"whi{s}", [P, KT, UW], F32R) for s in range(2)]
        wlo = [place(f"wlo{s}", [P, KT, UW], F32R) for s in range(2)]
        k_hi = place("k_hi", [P, 5, TOK], F32R)
        k_lo = place("k_lo", [P, 5, TOK], F32R)
        v_hi = place("v_hi", [P, 4, 640], F32R)
        v_lo = place("v_lo", [P, 4, 640], F32R)
        scr_at = at[0]
        scr = [place(f"scr{i}", [P, TOK], F32) for i in range(6)]
        pt_hi = [place(f"pt_hi{i}", [P, 4, P], F32R, scr_at + (2 + i) * 4 * TOK) for i in range(2)]
        pt_lo = [place(f"pt_lo{i}", [P, 4, P], F32R, scr_at + (4 + i) * 4 * TOK) for i in range(2)]
        cst = place("cst", [P, C_COLS], F32)
        ones = place("ones", [P, P], F32)
        vec = place("vec", [P, DEPTH, V_COLS], F32)
        bm = place("bm", [P, DEPTH * 72], F32)
        mod = place("mod", [P, DEPTH * 72, 2], F32)
        cs = place("cs", [P, KT, 2], F32)
        amul = place("amul", [P, KT, 2], F32)
        gate = place("gate", [P, KT, 2], F32)
        eps = place("eps", [P, 1], F32)
        nmax = place("nmax", [P, 64], F32)
        lsum = place("lsum", [P, 64], F32)
        linv = place("linv", [P, 64], F32)
        oss = place("oss", [P, 8], F32)
        flag = place("flag", [P, 1], F32)
        assert at[0] <= nc.sbuf_usable_end, at[0]

        ident = cst[:, C_ID:C_ID + P]
        blk = cst[:, C_BLK:C_BLK + P]
        rot = cst[:, C_ROT:C_ROT + P]
        cosv = cst[:, C_COS:C_COS + LAT]
        sinv = cst[:, C_SIN:C_SIN + LAT]

        bank = [ctx.enter_context(nc.psum_tensor(f"bank{b}", [P, TOK], F32)) for b in range(8)]

        const_in, x_in, bias_in, stored = sem("const_in"), sem("x_in"), sem("bias_in"), sem("stored")
        raw_in = [sem(f"raw_in{s}") for s in range(2)]
        w_hi = [sem(f"w_hi{s}") for s in range(2)]
        split = [sem(f"split{s}") for s in range(2)]
        half_mm = sem("half_mm")
        unit_mm = [sem(f"unit_mm{s}") for s in range(2)]
        mod_in = [sem(f"mod_in{s}") for s in range(2)]
        mod_mm = [sem(f"mod_mm{s}") for s in range(2)]
        mod_done = sem("mod_done")
        ready, cs_done, dchain, achain = sem("ready"), sem("cs_done"), sem("dchain"), sem("achain")
        silu_done, prod_done, hhid_done, hid_done = (sem(n) for n in ("silu_done", "prod_done", "hhid_done", "hid_done"))
        x_done, sq_done, acc_done, ssq_mm, sd_done = (sem(n) for n in ("x_done", "sq_done", "acc_done", "ssq_mm", "sd_done"))
        t_done, hf_done, hhi_done, h_done = (sem(n) for n in ("t_done", "hf_done", "hhi_done", "h_done"))
        qsq, qss_mm, qsd, qn_done, rot_mm, rope_done, q_hi_done, qk_done = (
            sem(n) for n in ("qsq", "qss_mm", "qsd", "qn_done", "rot_mm", "rope_done", "q_hi_done", "qk_done"))
        pj_hi, pj_done = sem("pj_hi"), sem("pj_done")
        bias_done, s_mm, nm_done, exp_done = (sem(n) for n in ("bias_done", "s_mm", "nm_done", "exp_done"))
        t_mm, pthi_done, ptlo_done, o_mm, o_done = (sem(n) for n in ("t_mm", "pthi_done", "ptlo_done", "o_mm", "o_done"))
        oss_done, orstd_done, onorm_done, yt_mm, y_hi_done, y_done = (
            sem(n) for n in ("oss_done", "orstd_done", "onorm_done", "yt_mm", "y_hi_done", "y_done"))
        f_done, g_masked = sem("f_done"), sem("g_masked")

        def tokens(layer, stage):
            return TOK if layer < DEPTH - 1 or stage < 2 else LAT

        norm_tok = [TOK] * 5 + [LAT] * 2

        def hf_before(n):
            return sum(KT * norm_tok[k] // LAT for k in range(n))

        def mod_after(i):
            return i >= 8

        def arrivals(u):
            extra = sum(3 for layer in range(DEPTH) for j in range(2)
                        if in_unit(layer) + j <= u and (in_unit(layer) + j) % 2 == u % 2)
            return 16 * (u // 2 + 1 + extra)

        def plain_tile(j, t, q_dst, k_dst, v_dst, b, Tq):
            if j < 5:
                return q_dst[:, 2 * (j - 3) + t, 0:Tq], bank[b + t][:, 0:Tq]
            if j < 7:
                return k_dst[:, 2 * (j - 5) + t, :], bank[b + t][:, :]
            c = (j - 7) * UW
            return v_dst[:, 2 * t:2 * t + 2, c:c + UW], bank[b + t][:, :].rearrange("p (a n) -> p a n", n=UW)

        block = ctx.enter_context(nc.Block())

        @block.sync
        def _(sp):
            sp.dma_start(x[:, :, 0:LAT], xT.rearrange("(k p) t -> p k t", p=P)).then_inc(x_in, 16)
            sp.dma_start(x[:, :, LAT:TOK], ctxT.rearrange("(k p) t -> p k t", p=P)).then_inc(x_in, 16)
            sp.dma_start(vec[:, :, :], vecs).then_inc(const_in, 16)
            sp.dma_start(bm[:, :], bmod).then_inc(const_in, 16)
            sp.dma_start(cst[:, :], consts).then_inc(const_in, 16)

            def load_unit(slot, gen, src):
                if not isinstance(gen, int) or gen > 0:
                    sp.wait_ge(split[slot], gen)
                sp.dma_start(raw[slot][:, 0:src.shape[1], :], src).then_inc(raw_in[slot], 16)

            def load_mod(slot, gen, col):
                if not isinstance(gen, int) or gen > 0:
                    sp.wait_ge(mod_mm[slot], gen)
                sp.dma_start(mraw[slot][:, :, :], col).then_inc(mod_in[slot], 16)

            mod_v = [w_mod[i].rearrange("(k p) n -> p k n", p=P) for i in range(DEPTH)]

            def mod_cols(m):
                layer, c = divmod(m * UW, N_MOD * D)
                return mod_v[layer][:, :, c:c + UW]

            def ffn(layer, second):
                w13 = (w13_2 if second else w13_1)[layer].rearrange("(k p) n -> p k n", p=P)
                w2 = (w2_2 if second else w2_1)[layer].rearrange("(k p) n -> p k n", p=P)
                u = ffn_unit(layer, second)
                pair = 0
                for n in CHUNKS:
                    def pair_loads(i):
                        for j, base in enumerate((0, FF)):
                            c = base + pair * UW
                            load_unit((u + j) % 2, i + (u + j) // 2, w13[:, :, bass.ds(i * UW + c, UW)])
                        if layer == 0 and not second:
                            for j in range(2):
                                m = MODS_FIRST + 2 * pair + j
                                load_mod(m % 2, i + m // 2, mod_v[0][:, :, bass.ds(i * (2 * UW) + m * UW, UW)])

                    if u == 0:
                        pair_loads(0)
                    with sp.Fori(1 if u == 0 else 0, n) as i:
                        pair_loads(i)
                    u += 2 * n
                    for j in range(W2_UNITS):
                        load_unit(u % 2, u // 2, w2[:, 2 * pair:2 * pair + 2 * n, j * UW:(j + 1) * UW])
                        u += 1
                    pair += n

            def mixer(layer):
                win = w_in[layer].rearrange("(k p) n -> p k n", p=P)
                u = in_unit(layer)
                for j in range(2):
                    s = u % 2
                    if u >= 2:
                        sp.wait_ge(split[s], u // 2)
                    for t in range(2):
                        for g in range(2):
                            c = QB_COL + HD * (2 * j + t + 4 * g)
                            to = t * P + g * HD
                            sp.dma_start(raw[s][:, :, to:to + HD], win[:, :, c:c + HD]).then_inc(raw_in[s], 16)
                    u += 1
                for c in (2048, 0, 256, 512, 768, 1024, 1280):
                    load_unit(u % 2, u // 2, win[:, :, c:c + UW])
                    u += 1
                wo = w_out[layer].rearrange("(k p) n -> p k n", p=P)
                for j in range(OUT_UNITS):
                    load_unit(u % 2, u // 2, wo[:, :, j * UW:(j + 1) * UW])
                    u += 1
                last = in_unit(layer) + IN_UNITS - 1
                sp.wait_ge(unit_mm[last % 2], last // 2 + 1)
                for qr in range(ROWS):
                    for kr in range(ROWS):
                        src = bass.AP(tensor=rpb.tensor,
                                      offset=layer * HEADS * RPB_H * RPB_W + (kr - qr + 7) * RPB_W - (GRID_W - WIN_W),
                                      ap=[[1, GRID_W], [RPB_H * RPB_W, HEADS], [1, GRID_W]])
                        p0 = GRID_W * (qr % 2)
                        sp.dma_start(bias[p0:p0 + GRID_W, qr // 2, :, kr, :], src).then_inc(bias_in, 16)
                if layer == 0:
                    for m in range(MOD_ATT0, MODS):
                        load_mod(m % 2, m // 2, mod_cols(m))

            for m in range(MODS_FIRST):
                load_mod(m % 2, m // 2, mod_cols(m))
            for layer in range(DEPTH):
                ffn(layer, False)
                mixer(layer)
                ffn(layer, True)
            sp.wait_ge(f_done, KT)
            sp.dma_start(outT.rearrange("(k p) t -> p k t", p=P), y_out[:, :, :]).then_inc(stored, 16)
            sp.wait_ge(stored, 16)

        @block.scalar
        def _(act):
            def hi_split(u, i=0):
                s = u % 2
                if u >= 2:
                    act.wait_ge(unit_mm[s], u // 2 + i)
                act.wait_ge(raw_in[s], arrivals(u) + i * 16)
                act.activation(whi[s][:, :, :], raw[s][:, :, :], ACT.Copy).then_inc(w_hi[s], 1)

            def squares(n, kts):
                T = norm_tok[n]
                for kt in kts:
                    if kt >= 3:
                        act.wait_ge(acc_done, (KT - 1) * n + kt - 2)
                    dst = scr[2] if kt == 0 else scr[kt % 2]
                    act.activation(dst[:, 0:T], x[:, kt, 0:T], ACT.Square).then_inc(sq_done, 1)

            def norm(n, shift):
                T = norm_tok[n]
                act.wait_ge(ssq_mm, n + 1)
                act.activation(scr[3][:, 0:T], bank[4][:, 0:T], ACT.Sqrt, bias=eps[:, 0:1],
                               scale=1.0 / D).then_inc(sd_done, 1)
                for kt in range(KT):
                    act.wait_ge(t_done, KT * n + kt + 1)
                    if n == len(norm_tok) - 1:
                        g = vec[:, 0, V_NF + kt:V_NF + kt + 1]
                        act.activation(y_out[:, kt, :], scr[kt % 2][:, 0:T], ACT.Copy,
                                       scale=g).then_inc(f_done, 1)
                        continue
                    if kt >= 2:
                        act.wait_ge(h_done, KT * n + kt - 1)
                    for c in range(T // LAT):
                        sl = slice(c * LAT, (c + 1) * LAT)
                        act.activation(scr[4 + kt % 2][:, sl], scr[kt % 2][:, sl], ACT.Identity,
                                       scale=amul[:, kt, c:c + 1],
                                       bias=mod[:, 8 * shift + kt, c:c + 1]).then_inc(hf_done, 1)

            def ffn(layer, second):
                T = tokens(layer, 2 * second)
                u = ffn_unit(layer, second)
                tile = HTILES * (2 * layer + second)
                xb = x_before(layer, 2 * second)
                for chunk, n in enumerate(CHUNKS):
                    with act.Fori(0, n) as i:
                        hi_split(u + 2, i)
                        for t in range(2):
                            if t == 0:
                                act.wait_ge(half_mm, i * 2 + (u + 2))
                            else:
                                act.wait_ge(unit_mm[(u + 1) % 2], i + ((u + 1) // 2 + 1))
                            act.activation(scr[t][:, 0:T], bank[2 + t][:, 0:T], ACT.Silu).then_inc(silu_done, 1)
                            act.wait_ge(prod_done, i * 2 + (TOKENS2 + tile + t + 1))
                            act.activation(hid_hi[:, bass.ds(i * 2 + t, 1), 0:T],
                                           scr[2 + t][:, 0:T].rearrange("p (a t) -> p a t", a=1),
                                           ACT.Copy).then_inc(hhid_done, 1)
                        hi_split(u + 3, i)
                    u += 2 * n
                    tile += 2 * n
                    for j in range(W2_UNITS):
                        update(u, j, xb, layer, 1 + 2 * second + layer * 3 if chunk == 2 else None)
                        u += 1
                    xb += KT

            def update(u, j, xb, layer, n):
                last = j == W2_UNITS - 1
                if not (last and n is not None) and u + 2 < UNITS:
                    hi_split(u + 2)
                if n is not None:
                    for t in range(2):
                        act.wait_ge(x_done, xb + 2 * j + t + 1)
                        squares(n, [2 * j + t])
                    if last and u + 2 < UNITS:
                        hi_split(u + 2)

            def mixer(layer):
                u = in_unit(layer)
                Tq = tokens(layer, 2)
                cb, pb = CHAINS * layer, PLAIN * layer

                def chain_tok(n):
                    return TOK if n == 4 else Tq

                def take(n):
                    T = chain_tok(n)
                    b = (0, 1, 2, 3, 0)[n]
                    if n >= 2:
                        act.wait_ge(qk_done, cb + n - 1)
                    uu = u + (0, 0, 1, 1, 2)[n]
                    if n % 2 == 0:
                        act.wait_ge(half_mm, uu + 1)
                    else:
                        act.wait_ge(unit_mm[uu % 2], uu // 2 + 1)
                    act.activation(scr[n % 2][:, 0:T], bank[b][:, 0:T], ACT.Copy).then_inc(achain, 1)
                    act.activation(scr[2 + n % 2][:, 0:T], bank[b][:, 0:T], ACT.Square).then_inc(qsq, 1)

                def deviation(n):
                    T = chain_tok(n)
                    act.wait_ge(qss_mm, cb + n + 1)
                    act.activation(scr[2 + n % 2][:, 0:T], bank[4 + n % 2][:, 0:T], ACT.Sqrt,
                                   bias=eps[:, 0:1], scale=1.0 / HD).then_inc(qsd, 1)

                def chain_hi(n):
                    T = chain_tok(n)
                    act.wait_ge(rope_done, cb + n + 1)
                    dst = k_hi[:, 4, 0:T] if n == 4 else hid_hi[:, 4 + n, 0:T]
                    act.activation(dst, scr[n % 2][:, 0:T], ACT.Copy).then_inc(q_hi_done, 1)

                def plain(j, t, dst, src):
                    if t == 0:
                        act.wait_ge(half_mm, u + j + 1)
                    else:
                        act.wait_ge(unit_mm[(u + j) % 2], (u + j) // 2 + 1)
                    act.activation(dst, src, ACT.Copy).then_inc(pj_hi, 1)

                take(0)
                take(1)
                hi_split(u + 2)
                deviation(0)
                deviation(1)
                hi_split(u + 3)
                chain_hi(0)
                chain_hi(1)
                take(2)
                take(3)
                deviation(2)
                deviation(3)
                hi_split(u + 4)
                chain_hi(2)
                chain_hi(3)
                take(4)
                plain(2, 1, v_hi[:, :, 512:640], bank[1][:, :].rearrange("p (a n) -> p a n", n=P))
                plain(3, 0, hid_hi[:, 0, 0:Tq], bank[2][:, 0:Tq])
                deviation(4)
                plain(3, 1, hid_hi[:, 1, 0:Tq], bank[3][:, 0:Tq])
                hi_split(u + 5)
                chain_hi(4)
                for j in range(4, IN_UNITS):
                    b = 2 * (j % 2)
                    for t in range(2):
                        plain(j, t, *plain_tile(j, t, hid_hi, k_hi, v_hi, b, Tq))
                    hi_split(u + j + 2)

                work = items(layer)
                i0 = ITEMS0[layer]
                for i in range(len(work) + 1):
                    if i < len(work):
                        N = TOK if work[i][1] < 2 else TOK - LAT
                        n = i0 + i
                        act.wait_ge(nm_done, n + 1)
                        if i >= 2:
                            act.wait_ge(t_mm, n - 1)
                        act.activation(scr[i % 2][:, 0:N], bank[i % 2][:, 0:N], ACT.Exp,
                                       bias=nmax[:, i:i + 1], scale=-1.0,
                                       accum_out=lsum[:, i:i + 1]).then_inc(exp_done, 1)
                    if i >= 1:
                        k = i - 1
                        n = i0 + k
                        kk = 4 if work[k][1] < 2 else 2
                        act.wait_ge(t_mm, n + 1)
                        if k >= 2:
                            act.wait_ge(o_mm, n - 1)
                        act.activation(pt_hi[k % 2][:, 0:kk, :],
                                       bank[2 + k % 2][:, 0:kk * P].rearrange("p (a n) -> p a n", n=P),
                                       ACT.Copy).then_inc(pthi_done, 1)

                tts = Tq // P
                act.wait_ge(o_done, ITEMS0[layer + 1])
                oss0 = sum(2 * tokens(i, 2) // P for i in range(layer))
                for g in range(2):
                    for tt in range(tts):
                        if g * tts + tt >= 2:
                            act.wait_ge(oss_done, oss0 + g * tts + tt - 1)
                        act.activation(scr[(g * tts + tt) % 2][:, :], o[:, tt, 512 * g:512 * (g + 1)], ACT.Square,
                                       accum_out=oss[:, g * 4 + tt:g * 4 + tt + 1]).then_inc(oss_done, 1)
                act.wait_ge(oss_done, oss0 + 2 * tts)
                for g in range(2):
                    act.activation(oss[:, 4 * g:4 * g + tts], oss[:, 4 * g:4 * g + tts], ACT.Sqrt,
                                   bias=eps[:, 0:1], scale=1.0 / (HEADS * HD)).then_inc(orstd_done, 1)
                for ct in range(KT):
                    n = KT * layer + ct
                    act.wait_ge(yt_mm, n + 1)
                    act.activation(hid_hi[:, ct, 0:Tq], bank[ct % 4][:, 0:Tq], ACT.Copy,
                                   scale=vec[:, layer, V_GO + ct:V_GO + ct + 1]).then_inc(y_hi_done, 1)
                uo = out_unit(layer)
                xb = x_before(layer, 1)
                for j in range(OUT_UNITS):
                    update(uo + j, j, xb, layer, 3 * layer + 2)

            act.wait_ge(const_in, 48)
            act.activation(cs[:, :, :], vec[:, 0, V_C:V_C + 16].rearrange("p (k c) -> p k c", c=2),
                           ACT.Silu).then_inc(cs_done, 1)
            act.wait_ge(x_in, 32)
            squares(0, range(KT))
            hi_split(0)
            act.wait_ge(ready, 1)
            norm(0, 0)
            hi_split(1)
            for layer in range(DEPTH):
                ffn(layer, False)
                norm(3 * layer + 1, 9 * layer + 3)
                mixer(layer)
                norm(3 * layer + 2, 9 * layer + 6)
                ffn(layer, True)
                norm(3 * layer + 3, 9 * (layer + 1))

        @block.vector
        def _(dve):
            links = [0]

            def link(ins):
                links[0] += 1
                ins.then_inc(dchain, 1)
                dve.wait_ge(dchain, links[0])

            def lo_split(u, i=0):
                s = u % 2
                dve.wait_ge(w_hi[s], u // 2 + 1 + i)
                dve.tensor_tensor(wlo[s][:, :, :], raw[s][:, :, :], whi[s][:, :, :].bitcast(F32),
                                  ALU.subtract).then_inc(split[s], 1)

            def add_squares(n, kts):
                T = norm_tok[n]
                for kt in kts:
                    if kt == 0:
                        continue
                    dve.wait_ge(sq_done, KT * n + kt + 1)
                    if kt >= 2:
                        dve.wait_ge(acc_done, (KT - 1) * n + kt - 1)
                    dve.tensor_tensor(scr[2][:, 0:T], scr[2][:, 0:T], scr[kt % 2][:, 0:T],
                                      ALU.add).then_inc(acc_done, 1)

            def mod_out(m, i=0):
                s = m % 2
                dve.wait_ge(mod_mm[s], m // 2 + 1 + i)
                a = i * 4 + 2 * m
                dve.tensor_tensor(mod[:, bass.ds(a, 2), :] if not isinstance(i, int) else mod[:, 2 * m:2 * m + 2, :],
                                  bank[6 + s][:, 0:4].rearrange("p (a c) -> p a c", c=2),
                                  (bm[:, bass.ds(a, 2)] if not isinstance(i, int) else bm[:, 2 * m:2 * m + 2])
                                  .unsqueeze(2).broadcast_to([P, 2, 2]), ALU.add).then_inc(mod_done, 1)

            def prepare(layer, col, chunk):
                dve.wait_ge(mod_done, min(MODS, 4 * (9 * layer + chunk + 2)))
                c = 8 * (9 * layer + chunk + 1)
                link(dve.scalar_tensor_tensor(
                    out=amul[:, :, :], in0=mod[:, c:c + 8, :], scalar=1.0,
                    in1=vec[:, layer, col:col + 8].unsqueeze(2).broadcast_to([P, 8, 2]),
                    op0=ALU.add, op1=ALU.mult))

            def prepare_gate(layer, chunk, factor):
                dve.wait_ge(mod_done, 4 * (9 * layer + chunk + 1))
                c = 8 * (9 * layer + chunk)
                link(dve.tensor_scalar(gate[:, :, :], mod[:, c:c + 8, :], factor, None, ALU.mult))

            def norm(n):
                T = norm_tok[n]
                dve.wait_ge(sd_done, n + 1)
                link(dve.reciprocal(scr[3][:, 0:T], scr[3][:, 0:T]))
                final = n == len(norm_tok) - 1
                for kt in range(KT + 1):
                    if kt < KT:
                        if kt >= 2:
                            if final:
                                dve.wait_ge(f_done, kt - 1)
                            else:
                                dve.wait_ge(hf_done, hf_before(n) + (T // LAT) * (kt - 1))
                        dve.tensor_tensor(scr[kt % 2][:, 0:T], x[:, kt, 0:T], scr[3][:, 0:T],
                                          ALU.mult).then_inc(t_done, 1)
                    if kt >= 1 and not final:
                        k = kt - 1
                        dve.wait_ge(hhi_done, KT * n + k + 1)
                        dve.tensor_tensor(h_lo[:, k, 0:T], scr[4 + k % 2][:, 0:T], h_hi[:, k, 0:T].bitcast(F32),
                                          ALU.subtract).then_inc(h_done, 1)

            def ffn(layer, second):
                T = tokens(layer, 2 * second)
                u = ffn_unit(layer, second)
                tile = HTILES * (2 * layer + second)
                xb = x_before(layer, 2 * second)
                mods = layer == 0 and not second
                m = MODS_FIRST
                for chunk, n in enumerate(CHUNKS):
                    with dve.Fori(0, n) as i:
                        if mods:
                            mod_out(m, i)
                            mod_out(m + 1, i)
                        lo_split(u + 2, i)
                        for t in range(2):
                            dve.wait_ge(silu_done, i * 2 + (TOKENS2 + tile + t + 1))
                            dve.tensor_tensor(scr[2 + t][:, 0:T], scr[t][:, 0:T], bank[t][:, 0:T],
                                              ALU.mult).then_inc(prod_done, 1)
                            dve.wait_ge(hhid_done, i * 2 + (tile + t + 1))
                            one = "p (a t) -> p a t"
                            dve.tensor_tensor(hid_lo[:, bass.ds(i * 2 + t, 1), 0:T],
                                              scr[2 + t][:, 0:T].rearrange(one, a=1),
                                              hid_hi[:, bass.ds(i * 2 + t, 1), 0:T].bitcast(F32),
                                              ALU.subtract).then_inc(hid_done, 1)
                        lo_split(u + 3, i)
                    u += 2 * n
                    tile += 2 * n
                    m += 2 * n
                    if chunk == 0:
                        prepare_gate(layer, 2 + 6 * second, 0.5)
                    for j in range(W2_UNITS):
                        update(u, j, (4, 5) if j % 2 == 0 else (2, 3), T,
                               1 + 2 * second + layer * 3 if chunk == 2 else None)
                        u += 1
                    xb += KT

            def update(u, j, banks, T, n):
                for t in range(2):
                    if t == 0:
                        dve.wait_ge(half_mm, u + 1)
                    else:
                        dve.wait_ge(unit_mm[u % 2], u // 2 + 1)
                    kt = 2 * j + t
                    for c in range(T // LAT):
                        sl = slice(c * LAT, (c + 1) * LAT)
                        ins = dve.scalar_tensor_tensor(out=x[:, kt, sl], in0=bank[banks[t]][:, sl],
                                                       scalar=gate[:, kt, c:c + 1], in1=x[:, kt, sl],
                                                       op0=ALU.mult, op1=ALU.add)
                    ins.then_inc(x_done, 1)
                last = j == W2_UNITS - 1
                if not (last and n is not None) and u + 2 < UNITS:
                    lo_split(u + 2)
                if n is not None:
                    add_squares(n, [2 * j, 2 * j + 1])
                    if last and u + 2 < UNITS:
                        lo_split(u + 2)

            def mixer(layer):
                u = in_unit(layer)
                Tq = tokens(layer, 2)
                cb, pb = CHAINS * layer, PLAIN * layer
                plains = [pb]

                def chain_tok(n):
                    return TOK if n == 4 else Tq

                def head_norm(n):
                    T = chain_tok(n)
                    col = V_KN if n == 4 else V_QN
                    dve.wait_ge(qsd, cb + n + 1)
                    link(dve.reciprocal(scr[2 + n % 2][:, 0:T], scr[2 + n % 2][:, 0:T]))
                    dve.scalar_tensor_tensor(out=scr[n % 2][:, 0:T], in0=scr[n % 2][:, 0:T],
                                             scalar=vec[:, layer, col:col + 1], in1=scr[2 + n % 2][:, 0:T],
                                             op0=ALU.mult, op1=ALU.mult).then_inc(qn_done, 1)

                def rope(n):
                    q, tmp = scr[n % 2][:, 0:LAT], scr[2 + n % 2][:, 0:LAT]
                    dve.wait_ge(rot_mm, cb + n + 1)
                    dve.tensor_tensor(tmp, bank[6 + n % 2][:, 0:LAT], sinv, ALU.mult)
                    link(dve.tensor_tensor(q, q, cosv, ALU.mult))
                    dve.tensor_tensor(q, q, tmp, ALU.add).then_inc(rope_done, 1)

                def chain_lo(n):
                    T = chain_tok(n)
                    dve.wait_ge(q_hi_done, cb + n + 1)
                    hi, lo = (k_hi[:, 4, 0:T], k_lo[:, 4, 0:T]) if n == 4 else (hid_hi[:, 4 + n, 0:T], hid_lo[:, 4 + n, 0:T])
                    dve.tensor_tensor(lo, scr[n % 2][:, 0:T], hi.bitcast(F32), ALU.subtract).then_inc(qk_done, 1)

                def plain(hi, lo, src):
                    plains[0] += 1
                    dve.wait_ge(pj_hi, plains[0])
                    dve.tensor_tensor(lo, src, hi.bitcast(F32), ALU.subtract).then_inc(pj_done, 1)

                def plain_of(j, t):
                    b = 2 * (j % 2)
                    hi, src = plain_tile(j, t, hid_hi, k_hi, v_hi, b, Tq)
                    lo, _ = plain_tile(j, t, hid_lo, k_lo, v_lo, b, Tq)
                    plain(hi, lo, src)

                lo_split(u + 2)
                head_norm(0)
                head_norm(1)
                lo_split(u + 3)
                rope(0)
                rope(1)
                chain_lo(0)
                chain_lo(1)
                head_norm(2)
                head_norm(3)
                lo_split(u + 4)
                rope(2)
                rope(3)
                chain_lo(2)
                chain_lo(3)
                plain(v_hi[:, :, 512:640], v_lo[:, :, 512:640], bank[1][:, :].rearrange("p (a n) -> p a n", n=P))
                plain(hid_hi[:, 0, 0:Tq], hid_lo[:, 0, 0:Tq], bank[2][:, 0:Tq])
                head_norm(4)
                plain(hid_hi[:, 1, 0:Tq], hid_lo[:, 1, 0:Tq], bank[3][:, 0:Tq])
                lo_split(u + 5)
                rope(4)
                chain_lo(4)
                for j in range(4, IN_UNITS):
                    plain_of(j, 0)
                    plain_of(j, 1)
                    lo_split(u + j + 2)

                work = items(layer)
                i0 = ITEMS0[layer]
                m = MOD_ATT0
                for i in range(len(work) + 2):
                    if i < len(work):
                        grouped, tt, hd = work[i]
                        n = i0 + i
                        N = TOK if tt < 2 else TOK - LAT
                        dve.wait_ge(s_mm, n + 1)
                        S = bank[i % 2]
                        if not grouped and tt < 2:
                            dve.wait_ge(bias_done, layer + 1)
                            link(dve.scalar_tensor_tensor(
                                out=S[:, 0:LAT].rearrange("p (a b) -> p a b", a=ROWS), in0=bias[:, tt, hd, :, ::-1],
                                scalar=1.0 / SCALE, in1=S[:, 0:LAT].rearrange("p (a b) -> p a b", a=ROWS), op0=ALU.mult, op1=ALU.add))
                        dve.tensor_scalar(S[:, 0:N], S[:, 0:N], -SCALE, None, ALU.mult, ALU.min,
                                          accum_out=nmax[:, i:i + 1]).then_inc(nm_done, 1)
                    if 1 <= i <= len(work):
                        k = i - 1
                        kk = 4 if work[k][1] < 2 else 2
                        dve.wait_ge(pthi_done, i0 + k + 1)
                        dve.tensor_tensor(pt_lo[k % 2][:, 0:kk, :],
                                          bank[2 + k % 2][:, 0:kk * P].rearrange("p (a n) -> p a n", n=P),
                                          pt_hi[k % 2][:, 0:kk, :].bitcast(F32), ALU.subtract).then_inc(ptlo_done, 1)
                    if i >= 2:
                        k = i - 2
                        grouped, tt, hd = work[k]
                        link(dve.reciprocal(linv[:, k:k + 1], lsum[:, k:k + 1]))
                        dve.wait_ge(o_mm, i0 + k + 1)
                        c = 512 * grouped + HD * hd
                        dve.tensor_scalar(o[:, tt, c:c + HD], bank[4 + k % 2][:, 0:HD], linv[:, k:k + 1], None,
                                          ALU.mult).then_inc(o_done, 1)
                    if layer == 0 and mod_after(i) and m < MODS:
                        mod_out(m)
                        m += 1
                tts = Tq // P
                dve.wait_ge(orstd_done, 2 * layer + 2)
                for g in range(2):
                    link(dve.reciprocal(oss[:, 4 * g:4 * g + tts], oss[:, 4 * g:4 * g + tts]))
                for g in (1, 0):
                    for tt in range(tts):
                        dve.tensor_scalar(o[:, tt, 512 * g:512 * (g + 1)], o[:, tt, 512 * g:512 * (g + 1)],
                                          oss[:, 4 * g + tt:4 * g + tt + 1], None, ALU.mult).then_inc(onorm_done, 1)
                for ct in range(KT):
                    dve.wait_ge(y_hi_done, KT * layer + ct + 1)
                    dve.scalar_tensor_tensor(out=hid_lo[:, ct, 0:Tq], in0=bank[ct % 4][:, 0:Tq],
                                             scalar=vec[:, layer, V_GO + ct:V_GO + ct + 1],
                                             in1=hid_hi[:, ct, 0:Tq].bitcast(F32),
                                             op0=ALU.mult, op1=ALU.subtract).then_inc(y_done, 1)
                prepare_gate(layer, 5, 1.0)
                uo = out_unit(layer)
                for j in range(OUT_UNITS):
                    update(uo + j, j, (4, 5) if j % 2 == 0 else (6, 7), Tq, 3 * layer + 2)

            dve.memset(ones[:, :], 1.0)
            dve.memset(eps[:, 0:1], EPS).then_inc(ready, 1)
            dve.memset(lsum[:, :], 1.0).then_inc(silu_done, TOKENS2)
            dve.memset(nmax[:, :], 0.0).then_inc(prod_done, TOKENS2)
            dve.wait_ge(prod_done, TOKENS2)
            add_squares(0, range(KT))
            for m in range(MODS_FIRST):
                mod_out(m)
            prepare(0, V_N1, 0)
            lo_split(0)
            norm(0)
            lo_split(1)
            for layer in range(DEPTH):
                ffn(layer, False)
                prepare(layer, V_NMIX, 3)
                norm(3 * layer + 1)
                mixer(layer)
                prepare(layer, V_N2, 6)
                norm(3 * layer + 2)
                ffn(layer, True)
                if layer < DEPTH - 1:
                    prepare(layer + 1, V_N1, 0)
                norm(3 * layer + 3)

        @block.gpsimd
        def _(pool):
            def norm(n):
                T = norm_tok[n]
                for kt in range(KT):
                    pool.wait_ge(hf_done, hf_before(n) + (T // LAT) * (kt + 1))
                    pool.tensor_copy(h_hi[:, kt, 0:T], scr[4 + kt % 2][:, 0:T]).then_inc(hhi_done, 1)

            def mask(layer):
                pool.wait_ge(bias_in, 16 * ROWS * ROWS * (layer + 1))
                masks = 0
                for lo, sign, base in ((WIN_W, -1, GRID_W - 1 + WIN_W // 2), (0, 1, WIN_W // 2 - GRID_W)):
                    for qt in range(2):
                        for p0 in (0, GRID_W):
                            v = bias[p0:p0 + GRID_W, qt].rearrange("p h r c -> p (h r) c")[:, :, lo:lo + GRID_W - WIN_W]
                            pool.affine_select(out=v, in_=v, compare_op=ALU.is_ge, fill=-1e30,
                                               base=base + sign * lo,
                                               pattern=[[0, HEADS * ROWS], [sign, GRID_W - WIN_W]],
                                               channel_multiplier=sign).then_inc(g_masked, 1)
                    masks += 4
                    pool.wait_ge(g_masked, 8 * layer + masks)
                pool.memset(flag[:, :], 0.0).then_inc(bias_done, 1)

            norm(0)
            for layer in range(DEPTH):
                norm(3 * layer + 1)
                mask(layer)
                norm(3 * layer + 2)
                if layer < DEPTH - 1:
                    norm(3 * layer + 3)

        @block.tensor
        def _(pe):
            def product(out, terms, waits=None):
                n, of = terms
                for kt in range(n):
                    if waits is not None:
                        pe.wait_ge(waits[0], waits[1] + kt + 1)
                    a_hi, a_lo, b_hi, b_lo = of(kt)
                    pe.matmul(out, a_hi, b_hi, start=kt == 0, stop=False)
                    pe.matmul(out, a_hi, b_lo, start=False, stop=False)
                    mm = pe.matmul(out, a_lo, b_hi, start=False, stop=kt == n - 1)
                return mm

            def weights(s, c0, width, rhs_hi, rhs_lo, T, n=KT):
                return n, lambda kt: (whi[s][:, kt, c0:c0 + width], wlo[s][:, kt, c0:c0 + width],
                                      rhs_hi[:, kt, 0:T], rhs_lo[:, kt, 0:T])

            def mod_unit(m, i=0):
                s = m % 2
                if m >= 2:
                    pe.wait_ge(mod_done, m - 1 + i * 2)
                pe.wait_ge(mod_in[s], 16 * (m // 2 + 1) + i * 16)
                for t in range(2):
                    for kt in range(KT):
                        mm = pe.matmul(bank[6 + s][:, 2 * t:2 * t + 2], mraw[s][:, kt, t * P:(t + 1) * P],
                                       cs[:, kt, :], start=kt == 0, stop=kt == KT - 1)
                mm.then_inc(mod_mm[s], 1)

            def stats(n):
                T = norm_tok[n]
                pe.wait_ge(acc_done, (KT - 1) * (n + 1))
                pe.matmul(bank[4][:, 0:T], ones[:, :], scr[2][:, 0:T], start=True, stop=True).then_inc(ssq_mm, 1)

            def ffn(layer, second):
                T = tokens(layer, 2 * second)
                n_norm = 3 * layer + 2 * second
                u = ffn_unit(layer, second)
                tile = HTILES * (2 * layer + second)
                xb = x_before(layer, 2 * second)
                m = MODS_FIRST
                for chunk, n in enumerate(CHUNKS):
                    with pe.Fori(0, n) as i:
                        if layer == 0 and not second:
                            mod_unit(m, i)
                            mod_unit(m + 1, i)
                        for j in range(2):
                            s = (u + j) % 2
                            pe.wait_ge(split[s], i + ((u + j) // 2 + 1))
                            if j == 1 and xb > 0:
                                pe.wait_ge(x_done, xb)
                            for t in range(2):
                                pe.wait_ge((prod_done, silu_done)[j], i * 2 + (tile + t + 1))
                                mm = product(bank[2 * j + t][:, 0:T], weights(s, t * P, P, h_hi, h_lo, T),
                                             (h_done, KT * n_norm) if j == 0 and t == 0 else None)
                                mm.then_inc(half_mm if t == 0 else unit_mm[s], 1)
                    u += 2 * n
                    m += 2 * n
                    for j in range(W2_UNITS):
                        s = u % 2
                        pe.wait_ge(split[s], u // 2 + 1)
                        b = 4 if j % 2 == 0 else 2
                        for t in range(2):
                            if j >= 2:
                                pe.wait_ge(x_done, xb + 2 * (j - 2) + t + 1)
                            elif j == 0 and xb > 0:
                                pe.wait_ge(x_done, xb)
                            mm = product(bank[b + t][:, 0:T], weights(s, t * P, P, hid_hi, hid_lo, T, 2 * n),
                                         (hid_done, tile) if j == 0 and t == 0 else None)
                            mm.then_inc(half_mm if t == 0 else unit_mm[s], 1)
                        u += 1
                    tile += 2 * n
                    xb += KT

            def mixer(layer):
                u0 = in_unit(layer)
                Tq = tokens(layer, 2)
                cb, pb = CHAINS * layer, PLAIN * layer
                xb = x_before(layer, 1)

                def tile_of(j, t):
                    u = u0 + j
                    s = u % 2
                    if t == 0:
                        pe.wait_ge(split[s], u // 2 + 1)
                    b = 2 * (j % 2) + t
                    if j == 0:
                        pe.wait_ge(x_done, xb)
                    elif j == 2 and t == 0:
                        pe.wait_ge(qsq, cb + 1)
                    elif j == 2:
                        pe.wait_ge(qsq, cb + 2)
                    elif j == 3:
                        pe.wait_ge(qsq, cb + 3 + t)
                    elif j == 4 and t == 0:
                        pe.wait_ge(qsq, cb + 5)
                    elif j == 4:
                        pe.wait_ge(pj_done, pb + 1)
                    elif j >= 5:
                        pe.wait_ge(pj_done, pb + 2 * (j - 5) + t + 2)
                    wait = (h_done, KT * (3 * layer + 1)) if j == 0 and t == 0 else None
                    if j >= 7 or (j, t) == (2, 1):
                        c0, width, tts = (P, P, range(4)) if j == 2 else (0, UW, range(2 * t, 2 * t + 2))
                        for a, tt in enumerate(tts):
                            tk = slice(tt * P, (tt + 1) * P)
                            mm = product(bank[b][:, a * width:(a + 1) * width],
                                         (KT, lambda kt: (h_hi[:, kt, tk], h_lo[:, kt, tk],
                                                          whi[s][:, kt, c0:c0 + width], wlo[s][:, kt, c0:c0 + width])))
                    else:
                        T = Tq if j < 5 and j != 2 else TOK
                        mm = product(bank[b][:, 0:T], weights(s, t * P, P, h_hi, h_lo, T), wait)
                    mm.then_inc(half_mm if t == 0 else unit_mm[s], 1)

                def head_sums(n):
                    T = TOK if n == 4 else Tq
                    pe.wait_ge(qsq, cb + n + 1)
                    pe.matmul(bank[4 + n % 2][:, 0:T], blk, scr[2 + n % 2][:, 0:T], start=True,
                              stop=True).then_inc(qss_mm, 1)

                def rotate(n):
                    pe.wait_ge(qn_done, cb + n + 1)
                    pe.matmul(bank[6 + n % 2][:, 0:LAT], rot, scr[n % 2][:, 0:LAT], start=True,
                              stop=True).then_inc(rot_mm, 1)

                tile_of(0, 0)
                tile_of(0, 1)
                tile_of(1, 0)
                head_sums(0)
                head_sums(1)
                tile_of(1, 1)
                rotate(0)
                rotate(1)
                tile_of(2, 0)
                head_sums(2)
                head_sums(3)
                tile_of(2, 1)
                rotate(2)
                rotate(3)
                tile_of(3, 0)
                head_sums(4)
                tile_of(3, 1)
                rotate(4)
                for j in range(4, IN_UNITS):
                    tile_of(j, 0)
                    tile_of(j, 1)

                work = items(layer)
                i0 = ITEMS0[layer]
                pe.wait_ge(qk_done, cb + CHAINS)
                pe.wait_ge(pj_done, pb + PLAIN)
                m = MOD_ATT0
                for i in range(len(work) + 2):
                    if i < len(work):
                        grouped, tt, hd = work[i]
                        half = HD * (hd // 4 if grouped else hd % 2)
                        qt = 4 + hd % 4 if grouped else hd // 2
                        kt = 4 if grouped else hd // 2
                        ks = slice(0, TOK) if tt < 2 else slice(LAT, TOK)
                        N = ks.stop - ks.start
                        pp = slice(half, half + HD)
                        tk = slice(tt * P, (tt + 1) * P)
                        if i >= 2:
                            pe.wait_ge(exp_done, i0 + i - 1)
                        product(bank[i % 2][:, 0:N],
                                (1, lambda _: (hid_hi[pp, qt, tk], hid_lo[pp, qt, tk], k_hi[pp, kt, ks], k_lo[pp, kt, ks]))
                                ).then_inc(s_mm, 1)
                    if 1 <= i <= len(work):
                        k = i - 1
                        kk = 4 if work[k][1] < 2 else 2
                        pe.wait_ge(exp_done, i0 + k + 1)
                        if k >= 2:
                            pe.wait_ge(ptlo_done, i0 + k - 1)
                        for a in range(kk):
                            mm = pe.transpose(bank[2 + k % 2][:, a * P:(a + 1) * P], scr[k % 2][:, a * P:(a + 1) * P], ident)
                        mm.then_inc(t_mm, 1)
                    if i >= 2:
                        k = i - 2
                        grouped, tt, hd = work[k]
                        kk = 4 if tt < 2 else 2
                        c = 512 + HD * (hd // 4) if grouped else HD * hd
                        pe.wait_ge(ptlo_done, i0 + k + 1)
                        if k >= 2:
                            pe.wait_ge(o_done, i0 + k - 1)
                        product(bank[4 + k % 2][:, 0:HD],
                                (kk, lambda a: (pt_hi[k % 2][:, a, :], pt_lo[k % 2][:, a, :],
                                                v_hi[:, 4 - kk + a, c:c + HD], v_lo[:, 4 - kk + a, c:c + HD]))
                                ).then_inc(o_mm, 1)
                    if layer == 0 and mod_after(i) and m < MODS:
                        mod_unit(m)
                        m += 1
                tts = Tq // P
                n_on = sum(2 * tokens(i, 2) // P for i in range(layer))
                for c in range(KT):
                    ct = (c + 4) % KT
                    ct = c
                    if c >= 4:
                        pe.wait_ge(y_done, KT * layer + c - 3)
                    pe.wait_ge(onorm_done, n_on + 2 * tts)
                    for tt in range(tts):
                        mm = pe.transpose(bank[c % 4][:, tt * P:(tt + 1) * P], o[:, tt, ct * P:(ct + 1) * P], ident)
                    mm.then_inc(yt_mm, 1)
                for j in range(OUT_UNITS):
                    u = out_unit(layer) + j
                    s = u % 2
                    pe.wait_ge(split[s], u // 2 + 1)
                    b = 4 if j % 2 == 0 else 6
                    for t in range(2):
                        if j >= 2:
                            pe.wait_ge(x_done, xb + 2 * (j - 2) + t + 1)
                        elif j == 1 and t == 0 and layer == 0:
                            pe.wait_ge(mod_done, MODS)
                        mm = product(bank[b + t][:, 0:Tq], weights(s, t * P, P, hid_hi, hid_lo, Tq),
                                     (y_done, KT * layer) if j == 0 and t == 0 else None)
                        mm.then_inc(half_mm if t == 0 else unit_mm[s], 1)

            pe.wait_ge(ready, 1)
            pe.wait_ge(cs_done, 1)
            mod_unit(0)
            mod_unit(1)
            stats(0)
            for m in range(2, MODS_FIRST):
                mod_unit(m)
            for layer in range(DEPTH):
                ffn(layer, False)
                stats(3 * layer + 1)
                mixer(layer)
                stats(3 * layer + 2)
                ffn(layer, True)
                stats(3 * layer + 3)


def _constants():
    c = np.zeros((P, C_COLS), np.float32)
    r = np.arange(P)
    c[:, C_ID:C_ID + P] = np.eye(P, dtype=np.float32)
    c[:, C_BLK:C_BLK + P] = (r[:, None] // HD == r[None, :] // HD).astype(np.float32)
    for m in range(P):
        first = m % 32 < 16
        c[m + 16 if first else m - 16, C_ROT + m] = -1.0 if first else 1.0
    t = np.arange(LAT)
    inv = (np.float32(ROPE_THETA) ** (-np.arange(0, HD // 2, 2, dtype=np.float32) / np.float32(HD // 2))).astype(np.float32)
    for m in range(P):
        d = m % HD
        pos = (t // GRID_W if d < HD // 2 else t % GRID_W).astype(np.float32)
        ang = pos * inv[d % 16]
        c[m, C_COS:C_COS + LAT] = np.cos(ang)
        c[m, C_SIN:C_SIN + LAT] = np.sin(ang)
    return c


def kernel(x, c, ctx, c_ctx, w_mod, b_mod, norm_ffn1, ffn1_w13, ffn1_w2, norm_mix, w_in, na_rpb,
           gqa_q_norm, gqa_k_norm, out_norm_a, out_norm_b, w_out, norm_ffn2, ffn2_w13, ffn2_w2, norm_f):
    import concourse.bacc as bacc
    from concourse.bass_utils import run_bass_kernel_spmd

    def columns(v):
        return np.asarray(v).reshape(-1, P).T

    per_layer = []
    for i in range(DEPTH):
        cond = np.stack([columns(c), columns(c_ctx)], axis=2).reshape(P, 2 * KT)
        head = [np.concatenate([g[i], g[i]]).reshape(P, 1) for g in (np.asarray(gqa_q_norm), np.asarray(gqa_k_norm))]
        per_layer.append(np.concatenate(
            [columns(norm_ffn1[i]), columns(norm_mix[i]), columns(norm_ffn2[i]), columns(out_norm_a[i]),
             columns(out_norm_b[i]), *head, columns(norm_f), cond], axis=1))
    arrays = {
        "xT": np.asarray(x)[0].T, "ctxT": np.asarray(ctx)[0].T,
        "vecs": np.stack(per_layer, axis=1), "bmod": columns(b_mod), "consts": _constants(),
        "w_mod": w_mod, "ffn1_w13": ffn1_w13, "ffn1_w2": ffn1_w2, "w_in": w_in, "rpb": np.asarray(na_rpb)[..., ::-1],
        "w_out": w_out, "ffn2_w13": ffn2_w13, "ffn2_w2": ffn2_w2,
    }
    arrays = {n: np.ascontiguousarray(a) for n, a in arrays.items()}
    nc = bacc.Bacc("TRN2", target_bir_lowering=False, num_devices=1)
    args = [nc.dram_tensor(n, a.shape, mybir.dt.from_np(a.dtype), kind="ExternalInput").ap() for n, a in arrays.items()]
    out = nc.dram_tensor("outT", (D, LAT), F32, kind="ExternalOutput").ap()
    build(nc, *args, out)
    r = run_bass_kernel_spmd(nc, [arrays], core_ids=[0])
    return np.ascontiguousarray(r.results[0]["outT"].T).reshape(1, LAT, D)
```

```python
from contextlib import ExitStack

import numpy as np

import concourse.bass as bass
from concourse import mybir

F32 = mybir.dt.float32
F32R = mybir.dt.float32r
ACT = mybir.ActivationFunctionType
ALU = mybir.AluOpType

P = 128
D = 1024
KT = D // P
DEPTH = 2
LAT = 256
TOK = 512
HD = 64
HEADS = 8
GRID_W = 64
ROWS = LAT // GRID_W
WIN_W = 16
RPB_H, RPB_W = 15, 31
FF = 2816
N_MOD = 9
EPS = 1e-6
SCALE = HD ** -0.5
ROPE_THETA = 10000.0
UW = 256
IN_W = 2304
QB_COL = 1536

CHUNKS = (4, 4, 3)
W2_UNITS = D // UW
FFN_UNITS = 2 * sum(CHUNKS) + W2_UNITS * len(CHUNKS)
IN_UNITS = IN_W // UW
OUT_UNITS = D // UW
LAYER_UNITS = 2 * FFN_UNITS + IN_UNITS + OUT_UNITS
UNITS = DEPTH * LAYER_UNITS
HTILES = FF // P
X_PER_FFN = KT * len(CHUNKS)

MODS = DEPTH * N_MOD * D // UW
MODS_FIRST = 2 * D // UW

CHAINS = 5
PLAIN = 13

V_N1, V_NMIX, V_N2, V_GO, V_QN, V_KN, V_NF, V_C, V_COLS = 0, 8, 16, 24, 32, 33, 34, 42, 58
C_ID, C_BLK, C_ROT, C_COS, C_SIN, C_COLS = 0, 128, 256, 384, 640, 896

TOKENS2 = 2

MODS_BESIDE_IN = (5, 6, 7)
MODS_BESIDE_W2 = (4, 4, 2)


def mod_plan():
    plan, used = {}, [[], []]

    def take(place, slots):
        plan[place] = []
        for s in slots:
            m = MODS_FIRST + len(used[0]) + len(used[1])
            if m < MODS:
                plan[place].append((m, s, len(used[s]), used[s][-1] if used[s] else None))
                used[s].append(m)

    plan["first"] = [(m, m // 2 % 2, 0, None) for m in range(MODS_FIRST)]
    for layer, second in ((0, False), (0, True), (1, False)):
        if second:
            take("w_in", [j % 2 for j in MODS_BESIDE_IN])
            take("w_out", [j % 2 for j in range(W2_UNITS)])
        for chunk, n in enumerate(CHUNKS):
            take(("pairs", layer, second, chunk), [1] * n)
            take(("w2", layer, second, chunk), [j % 2 for j in range(MODS_BESIDE_W2[chunk])])
    return plan


PLAN = mod_plan()


def planned(*place):
    return PLAN.get(place[0] if len(place) == 1 else place, [])


def paired(place):
    assert len({(m - i, s, g - i) for i, (m, s, g, _) in enumerate(planned(*place))}) <= 1
    return planned(*place)[0] if planned(*place) else None


def ffn_unit(layer, second):
    return layer * LAYER_UNITS + (FFN_UNITS + IN_UNITS + OUT_UNITS if second else 0)


def in_unit(layer):
    return layer * LAYER_UNITS + FFN_UNITS


def out_unit(layer):
    return in_unit(layer) + IN_UNITS


def x_before(layer, stage):
    return layer * (2 * X_PER_FFN + KT) + (0, X_PER_FFN, X_PER_FFN + KT)[stage]


def items(layer):
    tiles = range(4) if layer < DEPTH - 1 else range(2)
    return [(g, tt, h) for g in (True, False) for tt in tiles for h in range(HEADS)]


ITEMS0 = (0, len(items(0)), len(items(0)) + len(items(1)))


def build(nc, xT, ctxT, vecs, bmod, consts, w_mod, w13_1, w2_1, w_in, rpb, w_out, w13_2, w2_2, outT):
    ctx = ExitStack()
    with ctx:
        def sem(name):
            return ctx.enter_context(nc.semaphore(name))

        at = [16512]

        def place(name, shape, dt, where=None):
            size = -(-4 * int(np.prod(shape[1:])) // 32) * 32
            if where is None:
                where = at[0]
                at[0] += size
            return nc.alloc_sbuf_tensor_at(name, shape, dt, offset=where)

        x = place("x", [P, KT, TOK], F32)
        h_hi_at = at[0]
        h_hi = place("h_hi", [P, KT, TOK], F32R)
        h_lo_at = at[0]
        h_lo = place("h_lo", [P, KT, TOK], F32R)
        o = place("o", [P, 4, D], F32, h_hi_at)
        y_out = place("y_out", [P, KT, LAT], F32, h_hi_at)
        bias = place("bias", [P, 2, HEADS, ROWS, GRID_W], F32, h_lo_at)
        first_at = at[0]
        hid_hi = place("hid_hi", [P, 8, TOK], F32R)
        hid_lo = place("hid_lo", [P, 8, TOK], F32R)
        xn = place("xn", [P, KT, TOK], F32, first_at)
        hf = place("hf", [P, KT, TOK], F32, first_at + 4 * 8 * TOK)
        k_hi = place("k_hi", [P, 5, TOK], F32R)
        k_lo = place("k_lo", [P, 5, TOK], F32R)
        v_hi = place("v_hi", [P, 4, 640], F32R)
        v_lo = place("v_lo", [P, 4, 640], F32R)
        mfirst = [place(f"mfirst{m}", [P, KT, UW], F32, first_at + m * 4 * KT * UW) for m in range(MODS_FIRST)]
        assert first_at + MODS_FIRST * 4 * KT * UW <= at[0]
        raw = [place(f"raw{s}", [P, KT, UW], F32) for s in range(2)]
        mraw = [place(f"mraw{s}", [P, KT, UW], F32) for s in range(2)]
        whi = [place(f"whi{s}", [P, KT, UW], F32R) for s in range(2)]
        wlo = [place(f"wlo{s}", [P, KT, UW], F32R) for s in range(2)]
        scr_at = at[0]
        scr = [place(f"scr{i}", [P, TOK], F32) for i in range(6)]
        pt_hi = [place(f"pt_hi{i}", [P, 4, P], F32R, scr_at + (2 + i) * 4 * TOK) for i in range(2)]
        pt_lo = [place(f"pt_lo{i}", [P, 4, P], F32R, scr_at + (4 + i) * 4 * TOK) for i in range(2)]
        cst = place("cst", [P, C_COLS], F32)
        ones = place("ones", [P, P], F32)
        vec = place("vec", [P, DEPTH, V_COLS], F32)
        bm = place("bm", [P, DEPTH * 72], F32)
        mod = place("mod", [P, DEPTH * 72, 2], F32)
        cs = place("cs", [P, KT, 2], F32)
        amul = place("amul", [P, KT, 2], F32)
        gate = place("gate", [P, KT, 2], F32)
        macc = [place(f"macc{s}", [P, 2, UW], F32) for s in range(2)]
        eps = place("eps", [P, 1], F32)
        rms = place("rms", [P, 8, 4], F32)
        warm = place("warm", [P, 32], F32)
        nmax = place("nmax", [P, 64], F32)
        lsum = place("lsum", [P, 64], F32)
        linv = place("linv", [P, 64], F32)
        oss = place("oss", [P, 8], F32)
        flag = place("flag", [P, 1], F32)
        assert at[0] <= nc.sbuf_usable_end, at[0]

        ident = cst[:, C_ID:C_ID + P]
        blk = cst[:, C_BLK:C_BLK + P]
        rot = cst[:, C_ROT:C_ROT + P]
        cosv = cst[:, C_COS:C_COS + LAT]
        sinv = cst[:, C_SIN:C_SIN + LAT]

        bank = [ctx.enter_context(nc.psum_tensor(f"bank{b}", [P, TOK], F32)) for b in range(8)]

        const_in, x_in, bias_in, stored = sem("const_in"), sem("x_in"), sem("bias_in"), sem("stored")
        raw_in = [sem(f"raw_in{s}") for s in range(2)]
        w_hi = [sem(f"w_hi{s}") for s in range(2)]
        split = [sem(f"split{s}") for s in range(2)]
        half_mm = sem("half_mm")
        unit_mm = [sem(f"unit_mm{s}") for s in range(2)]
        mfirst_in = [sem(f"mfirst_in{m}") for m in range(MODS_FIRST)]
        mod_in = [sem(f"mod_in{s}") for s in range(2)]
        mod_step, mod_mm, mod_done = sem("mod_step"), sem("mod_mm"), sem("mod_done")
        ready, cs_done, dchain, achain = sem("ready"), sem("cs_done"), sem("dchain"), sem("achain")
        silu_done, prod_done, hhid_done, hid_done = (sem(n) for n in ("silu_done", "prod_done", "hhid_done", "hid_done"))
        x_done, sq_done, acc_done, ssq_mm, sd_done = (sem(n) for n in ("x_done", "sq_done", "acc_done", "ssq_mm", "sd_done"))
        t_done, hf_done, hhi_act, hhi_pool, h_done = (
            sem(n) for n in ("t_done", "hf_done", "hhi_act", "hhi_pool", "h_done"))
        diag_done, rstd_mm = sem("diag_done"), sem("rstd_mm")
        qsq, qss_mm, qsd, qn_done, rot_mm, rope_done, q_hi_done, qk_done = (
            sem(n) for n in ("qsq", "qss_mm", "qsd", "qn_done", "rot_mm", "rope_done", "q_hi_done", "qk_done"))
        pj_hi, pj_done = sem("pj_hi"), sem("pj_done")
        bias_done, s_mm, nm_done, exp_done = (sem(n) for n in ("bias_done", "s_mm", "nm_done", "exp_done"))
        t_mm, pthi_done, ptlo_done, o_mm, o_done = (sem(n) for n in ("t_mm", "pthi_done", "ptlo_done", "o_mm", "o_done"))
        oss_done, orstd_done, onorm_done, yt_mm, y_hi_done, y_done = (
            sem(n) for n in ("oss_done", "orstd_done", "onorm_done", "yt_mm", "y_hi_done", "y_done"))
        f_done, g_masked = sem("f_done"), sem("g_masked")

        def tokens(layer, stage):
            return TOK if layer < DEPTH - 1 or stage < 2 else LAT

        norm_tok = [TOK] * 5 + [LAT] * 2

        POOL_KT = (1, 3, 5)
        AHEAD = 3

        def hi_before(n, k, pool):
            mine = [j for j in range(KT) if (j in POOL_KT) == pool]
            return n * len(mine) + sum(j <= k for j in mine)

        def hf_before(n):
            return sum(KT * norm_tok[k] // LAT for k in range(n))

        MSTEPS = 2 * KT

        def by_vector(m):
            return m >= MODS_FIRST or m % 2 == 1

        def mod_steps(m):
            return MSTEPS * sum(by_vector(k) for k in range(m))

        def arrivals(u):
            extra = sum(3 for layer in range(DEPTH) for j in range(2)
                        if in_unit(layer) + j <= u and (in_unit(layer) + j) % 2 == u % 2)
            return 16 * (u // 2 + 1 + extra)

        def plain_tile(j, t, q_dst, k_dst, v_dst, b, Tq):
            if j < 5:
                return q_dst[:, 2 * (j - 3) + t, 0:Tq], bank[b + t][:, 0:Tq]
            if j < 7:
                return k_dst[:, 2 * (j - 5) + t, :], bank[b + t][:, :]
            c = (j - 7) * UW
            return v_dst[:, 2 * t:2 * t + 2, c:c + UW], bank[b + t][:, :].rearrange("p (a n) -> p a n", n=UW)

        block = ctx.enter_context(nc.Block())

        @block.sync
        def _(sp):
            sp.dma_start(x[:, :, 0:LAT], xT.rearrange("(k p) t -> p k t", p=P)).then_inc(x_in, 16)
            sp.dma_start(x[:, :, LAT:TOK], ctxT.rearrange("(k p) t -> p k t", p=P)).then_inc(x_in, 16)
            sp.dma_start(vec[:, :, :], vecs).then_inc(const_in, 16)
            sp.dma_start(bm[:, :], bmod).then_inc(const_in, 16)
            sp.dma_start(cst[:, :], consts).then_inc(const_in, 16)

            def load_unit(slot, gen, src):
                if not isinstance(gen, int) or gen > 0:
                    sp.wait_ge(split[slot], gen)
                sp.dma_start(raw[slot][:, 0:src.shape[1], :], src).then_inc(raw_in[slot], 16)

            mod_v = [w_mod[i].rearrange("(k p) n -> p k n", p=P) for i in range(DEPTH)]

            def load_mod(job, i=0):
                m, s, _, prev = job
                if not isinstance(i, int):
                    sp.wait_ge(mod_step, i * MSTEPS + mod_steps(m))
                elif prev is not None:
                    sp.wait_ge(mod_step, mod_steps(prev + 1))
                lay, c = divmod(m * UW, N_MOD * D)
                cols = slice(c, c + UW) if isinstance(i, int) else bass.ds(i * UW + c, UW)
                sp.dma_start(mraw[s][:, :, :], mod_v[lay][:, :, cols]).then_inc(mod_in[s], 16)

            def ffn(layer, second):
                w13 = (w13_2 if second else w13_1)[layer].rearrange("(k p) n -> p k n", p=P)
                w2 = (w2_2 if second else w2_1)[layer].rearrange("(k p) n -> p k n", p=P)
                u = ffn_unit(layer, second)
                pair = 0
                for chunk, n in enumerate(CHUNKS):
                    job = paired(("pairs", layer, second, chunk))

                    def pair_loads(i):
                        for j, base in enumerate((0, FF)):
                            c = base + pair * UW
                            load_unit((u + j) % 2, i + (u + j) // 2, w13[:, :, bass.ds(i * UW + c, UW)])
                        if job:
                            load_mod(job, i)

                    if u == 0:
                        for j, base in enumerate((0, FF)):
                            sp.dma_start(raw[j][:, :, :], w13[:, :, base:base + UW]).then_inc(raw_in[j], 16)
                        load_mod(job, 0)
                    with sp.Fori(1 if u == 0 else 0, n) as i:
                        pair_loads(i)
                    u += 2 * n
                    for j in range(W2_UNITS):
                        load_unit(u % 2, u // 2, w2[:, 2 * pair:2 * pair + 2 * n, j * UW:(j + 1) * UW])
                        for mod_job in planned("w2", layer, second, chunk)[j:j + 1]:
                            load_mod(mod_job)
                        u += 1
                    pair += n

            def mixer(layer):
                win = w_in[layer].rearrange("(k p) n -> p k n", p=P)
                u = in_unit(layer)
                for j in range(2):
                    s = u % 2
                    if u >= 2:
                        sp.wait_ge(split[s], u // 2)
                    for t in range(2):
                        for g in range(2):
                            c = QB_COL + HD * (2 * j + t + 4 * g)
                            to = t * P + g * HD
                            sp.dma_start(raw[s][:, :, to:to + HD], win[:, :, c:c + HD]).then_inc(raw_in[s], 16)
                    u += 1
                for j, c in enumerate((2048, 0, 256, 512, 768, 1024, 1280), 2):
                    load_unit(u % 2, u // 2, win[:, :, c:c + UW])
                    if layer == 0 and j in MODS_BESIDE_IN:
                        load_mod(planned("w_in")[MODS_BESIDE_IN.index(j)])
                    u += 1
                last = in_unit(layer) + IN_UNITS - 1
                wo = w_out[layer].rearrange("(k p) n -> p k n", p=P)

                def out_loads(js):
                    for j in js:
                        uo = out_unit(layer) + j
                        load_unit(uo % 2, uo // 2, wo[:, :, j * UW:(j + 1) * UW])
                        if layer == 0:
                            load_mod(planned("w_out")[j])

                out_loads(range(2))
                sp.wait_ge(unit_mm[last % 2], last // 2 + 1)
                for qr in range(ROWS):
                    for kr in range(ROWS):
                        src = bass.AP(tensor=rpb.tensor,
                                      offset=layer * HEADS * RPB_H * RPB_W + (kr - qr + 7) * RPB_W - (GRID_W - WIN_W),
                                      ap=[[1, GRID_W], [RPB_H * RPB_W, HEADS], [1, GRID_W]])
                        p0 = GRID_W * (qr % 2)
                        sp.dma_start(bias[p0:p0 + GRID_W, qr // 2, :, kr, :], src).then_inc(bias_in, 16)
                out_loads(range(2, OUT_UNITS))

            for m in range(MODS_FIRST):
                sp.dma_start(mfirst[m][:, :, :], mod_v[0][:, :, m * UW:(m + 1) * UW]).then_inc(mfirst_in[m], 16)
            for layer in range(DEPTH):
                ffn(layer, False)
                mixer(layer)
                ffn(layer, True)
            sp.wait_ge(f_done, KT)
            sp.dma_start(outT.rearrange("(k p) t -> p k t", p=P), y_out[:, :, :]).then_inc(stored, 16)
            sp.wait_ge(stored, 16)

        @block.scalar
        def _(act):
            def hi_split(u, i=0):
                s = u % 2
                if u >= 2:
                    act.wait_ge(unit_mm[s], u // 2 + i)
                act.wait_ge(raw_in[s], arrivals(u) + i * 16)
                act.activation(whi[s][:, :, :], raw[s][:, :, :], ACT.Copy).then_inc(w_hi[s], 1)

            def squares(n, kts):
                T = norm_tok[n]
                for kt in kts:
                    if kt >= 3:
                        act.wait_ge(acc_done, (KT - 1) * n + kt - 2)
                    dst = scr[2] if kt == 0 else scr[kt % 2]
                    act.activation(dst[:, 0:T], x[:, kt, 0:T], ACT.Square).then_inc(sq_done, 1)

            def root(n):
                nt = norm_tok[n] // P
                act.wait_ge(ssq_mm, n + 1)
                act.activation(rms[:, n, 0:nt], bank[4][:, 0:nt], ACT.Sqrt, bias=eps[:, 0:1],
                               scale=1.0 / D).then_inc(sd_done, 1)

            warmed = [0]

            def load_table(func):
                act.activation(warm[:, warmed[0]:warmed[0] + 1], eps[:, 0:1], func)
                warmed[0] += 1

            def norm(n, shift):
                T = norm_tok[n]
                if n > 0:
                    root(n)
                for kt in range(KT):
                    act.wait_ge(t_done, KT * n + kt + 1)
                    if n == len(norm_tok) - 1:
                        g = vec[:, 0, V_NF + kt:V_NF + kt + 1]
                        act.activation(y_out[:, kt, :], xn[:, kt, 0:T], ACT.Copy, scale=g).then_inc(f_done, 1)
                        continue
                    for c in range(T // LAT):
                        sl = slice(c * LAT, (c + 1) * LAT)
                        act.activation(hf[:, kt, sl], xn[:, kt, sl], ACT.Identity, scale=amul[:, kt, c:c + 1],
                                       bias=mod[:, 8 * shift + kt, c:c + 1]).then_inc(hf_done, 1)
                    if kt not in POOL_KT:
                        act.wait_ge(hf_done, hf_before(n) + (T // LAT) * (kt + 1))
                        act.activation(h_hi[:, kt, 0:T], hf[:, kt, 0:T], ACT.Copy).then_inc(hhi_act, 1)

            def ffn(layer, second):
                T = tokens(layer, 2 * second)
                u = ffn_unit(layer, second)
                tile = HTILES * (2 * layer + second)
                xb = x_before(layer, 2 * second)
                for chunk, n in enumerate(CHUNKS):
                    with act.Fori(0, n) as i:
                        hi_split(u + 2, i)
                        for t in range(2):
                            if t == 0:
                                act.wait_ge(half_mm, i * 2 + (u + 2))
                            else:
                                act.wait_ge(unit_mm[(u + 1) % 2], i + ((u + 1) // 2 + 1))
                            act.activation(scr[t][:, 0:T], bank[2 + t][:, 0:T], ACT.Silu).then_inc(silu_done, 1)
                            act.wait_ge(prod_done, i * 2 + (TOKENS2 + tile + t + 1))
                            act.activation(hid_hi[:, bass.ds(i * 2 + t, 1), 0:T],
                                           scr[2 + t][:, 0:T].rearrange("p (a t) -> p a t", a=1),
                                           ACT.Copy).then_inc(hhid_done, 1)
                        hi_split(u + 3, i)
                    u += 2 * n
                    tile += 2 * n
                    if chunk == len(CHUNKS) - 1:
                        load_table(ACT.Sqrt)
                    for j in range(W2_UNITS):
                        update(u, j, xb, layer, 1 + 2 * second + layer * 3 if chunk == 2 else None)
                        u += 1
                    xb += KT

            def update(u, j, xb, layer, n):
                last = j == W2_UNITS - 1
                if not (last and n is not None) and u + 2 < UNITS:
                    hi_split(u + 2)
                if n is not None:
                    for t in range(2):
                        act.wait_ge(x_done, xb + 2 * j + t + 1)
                        squares(n, [2 * j + t])
                    if last and u + 2 < UNITS:
                        hi_split(u + 2)

            def mixer(layer):
                u = in_unit(layer)
                Tq = tokens(layer, 2)
                cb, pb = CHAINS * layer, PLAIN * layer

                def chain_tok(n):
                    return TOK if n == 4 else Tq

                def take(n):
                    T = chain_tok(n)
                    b = (0, 1, 2, 3, 0)[n]
                    if n >= 2:
                        act.wait_ge(qk_done, cb + n - 1)
                    uu = u + (0, 0, 1, 1, 2)[n]
                    if n % 2 == 0:
                        act.wait_ge(half_mm, uu + 1)
                    else:
                        act.wait_ge(unit_mm[uu % 2], uu // 2 + 1)
                    act.activation(scr[n % 2][:, 0:T], bank[b][:, 0:T], ACT.Copy).then_inc(achain, 1)
                    act.activation(scr[2 + n % 2][:, 0:T], bank[b][:, 0:T], ACT.Square).then_inc(qsq, 1)

                def deviation(n):
                    T = chain_tok(n)
                    act.wait_ge(qss_mm, cb + n + 1)
                    act.activation(scr[2 + n % 2][:, 0:T], bank[4 + n % 2][:, 0:T], ACT.Sqrt,
                                   bias=eps[:, 0:1], scale=1.0 / HD).then_inc(qsd, 1)

                def chain_hi(n):
                    T = chain_tok(n)
                    act.wait_ge(rope_done, cb + n + 1)
                    dst = k_hi[:, 4, 0:T] if n == 4 else hid_hi[:, 4 + n, 0:T]
                    act.activation(dst, scr[n % 2][:, 0:T], ACT.Copy).then_inc(q_hi_done, 1)

                def plain(j, t, dst, src):
                    if t == 0:
                        act.wait_ge(half_mm, u + j + 1)
                    else:
                        act.wait_ge(unit_mm[(u + j) % 2], (u + j) // 2 + 1)
                    act.activation(dst, src, ACT.Copy).then_inc(pj_hi, 1)

                take(0)
                take(1)
                hi_split(u + 2)
                deviation(0)
                deviation(1)
                hi_split(u + 3)
                chain_hi(0)
                chain_hi(1)
                take(2)
                take(3)
                deviation(2)
                deviation(3)
                hi_split(u + 4)
                chain_hi(2)
                chain_hi(3)
                take(4)
                plain(2, 1, v_hi[:, :, 512:640], bank[1][:, :].rearrange("p (a n) -> p a n", n=P))
                plain(3, 0, hid_hi[:, 0, 0:Tq], bank[2][:, 0:Tq])
                deviation(4)
                plain(3, 1, hid_hi[:, 1, 0:Tq], bank[3][:, 0:Tq])
                hi_split(u + 5)
                chain_hi(4)
                for j in range(4, IN_UNITS):
                    b = 2 * (j % 2)
                    for t in range(2):
                        plain(j, t, *plain_tile(j, t, hid_hi, k_hi, v_hi, b, Tq))
                    hi_split(u + j + 2)
                load_table(ACT.Exp)

                work = items(layer)
                i0 = ITEMS0[layer]
                for i in range(len(work) + 1):
                    if i < len(work):
                        N = TOK if work[i][1] < 2 else TOK - LAT
                        n = i0 + i
                        act.wait_ge(nm_done, n + 1)
                        if i >= 2:
                            act.wait_ge(t_mm, n - 1)
                        act.activation(scr[i % 2][:, 0:N], bank[i % 2][:, 0:N], ACT.Exp,
                                       bias=nmax[:, i:i + 1], scale=-1.0,
                                       accum_out=lsum[:, i:i + 1]).then_inc(exp_done, 1)
                    if i >= 1:
                        k = i - 1
                        n = i0 + k
                        kk = 4 if work[k][1] < 2 else 2
                        act.wait_ge(t_mm, n + 1)
                        if k >= 2:
                            act.wait_ge(o_mm, n - 1)
                        act.activation(pt_hi[k % 2][:, 0:kk, :],
                                       bank[2 + k % 2][:, 0:kk * P].rearrange("p (a n) -> p a n", n=P),
                                       ACT.Copy).then_inc(pthi_done, 1)

                tts = Tq // P
                act.wait_ge(o_done, ITEMS0[layer + 1])
                oss0 = sum(2 * tokens(i, 2) // P for i in range(layer))
                for g in range(2):
                    for tt in range(tts):
                        if g * tts + tt >= 2:
                            act.wait_ge(oss_done, oss0 + g * tts + tt - 1)
                        act.activation(scr[(g * tts + tt) % 2][:, :], o[:, tt, 512 * g:512 * (g + 1)], ACT.Square,
                                       accum_out=oss[:, g * 4 + tt:g * 4 + tt + 1]).then_inc(oss_done, 1)
                act.wait_ge(oss_done, oss0 + 2 * tts)
                for g in range(2):
                    act.activation(oss[:, 4 * g:4 * g + tts], oss[:, 4 * g:4 * g + tts], ACT.Sqrt,
                                   bias=eps[:, 0:1], scale=1.0 / (HEADS * HD)).then_inc(orstd_done, 1)
                for ct in range(KT):
                    n = KT * layer + ct
                    act.wait_ge(yt_mm, n + 1)
                    act.activation(hid_hi[:, ct, 0:Tq], bank[ct % 4][:, 0:Tq], ACT.Copy,
                                   scale=vec[:, layer, V_GO + ct:V_GO + ct + 1]).then_inc(y_hi_done, 1)
                uo = out_unit(layer)
                xb = x_before(layer, 1)
                for j in range(OUT_UNITS):
                    update(uo + j, j, xb, layer, 3 * layer + 2)

            act.wait_ge(const_in, 48)
            act.activation(cs[:, :, :], vec[:, 0, V_C:V_C + 16].rearrange("p (k c) -> p k c", c=2),
                           ACT.Silu).then_inc(cs_done, 1)
            act.wait_ge(x_in, 32)
            squares(0, range(KT))
            act.wait_ge(ready, 1)
            root(0)
            hi_split(0)
            hi_split(1)
            norm(0, 0)
            for layer in range(DEPTH):
                load_table(ACT.Silu)
                ffn(layer, False)
                norm(3 * layer + 1, 9 * layer + 3)
                mixer(layer)
                norm(3 * layer + 2, 9 * layer + 6)
                load_table(ACT.Silu)
                ffn(layer, True)
                norm(3 * layer + 3, 9 * (layer + 1))

        @block.vector
        def _(dve):
            links = [0]

            def link(ins):
                links[0] += 1
                ins.then_inc(dchain, 1)
                dve.wait_ge(dchain, links[0])

            def lo_split(u, i=0):
                s = u % 2
                dve.wait_ge(w_hi[s], u // 2 + 1 + i)
                dve.tensor_tensor(wlo[s][:, :, :], raw[s][:, :, :], whi[s][:, :, :].bitcast(F32),
                                  ALU.subtract).then_inc(split[s], 1)

            def add_squares(n, kts):
                T = norm_tok[n]
                for kt in kts:
                    if kt == 0:
                        continue
                    dve.wait_ge(sq_done, KT * n + kt + 1)
                    if kt >= 2:
                        dve.wait_ge(acc_done, (KT - 1) * n + kt - 1)
                    dve.tensor_tensor(scr[2][:, 0:T], scr[2][:, 0:T], scr[kt % 2][:, 0:T],
                                      ALU.add).then_inc(acc_done, 1)

            def mod_sum(job, kts, i=0):
                m, s, g, _ = job
                src = mfirst[m] if m < MODS_FIRST else mraw[s]
                for kt in kts:
                    if kt == 0:
                        if m < MODS_FIRST:
                            dve.wait_ge(mfirst_in[m], 16)
                        else:
                            dve.wait_ge(mod_in[s], i * 16 + 16 * (g + 1))
                        if m >= MODS_FIRST:
                            dve.wait_ge(mod_mm, i + m)
                        elif m >= 4:
                            dve.wait_ge(mod_mm, m - 3)
                    for c in range(2):
                        if kt == 0:
                            dve.tensor_scalar(macc[s][:, c, :], src[:, kt, :], cs[:, kt, c:c + 1], None,
                                              ALU.mult).then_inc(mod_step, 1)
                            continue
                        dve.wait_ge(mod_step, i * MSTEPS + (mod_steps(m) + 2 * kt + c - 1))
                        dve.scalar_tensor_tensor(out=macc[s][:, c, :], in0=src[:, kt, :], scalar=cs[:, kt, c:c + 1],
                                                 in1=macc[s][:, c, :], op0=ALU.mult, op1=ALU.add).then_inc(mod_step, 1)

            def mod_out(m, b, i=0):
                dve.wait_ge(mod_mm, m + 1 + i)
                a = i * 2 + 2 * m
                cols = slice(a, a + 2) if isinstance(i, int) else bass.ds(a, 2)
                dve.tensor_tensor(mod[:, cols, :], bank[b][:, 0:4].rearrange("p (a c) -> p a c", c=2),
                                  bm[:, cols].unsqueeze(2).broadcast_to([P, 2, 2]), ALU.add).then_inc(mod_done, 1)

            def prepare(layer, col, chunk):
                dve.wait_ge(mod_done, min(MODS, 4 * (9 * layer + chunk + 2)))
                c = 8 * (9 * layer + chunk + 1)
                link(dve.scalar_tensor_tensor(
                    out=amul[:, :, :], in0=mod[:, c:c + 8, :], scalar=1.0,
                    in1=vec[:, layer, col:col + 8].unsqueeze(2).broadcast_to([P, 8, 2]),
                    op0=ALU.add, op1=ALU.mult))

            def prepare_gate(layer, chunk, factor):
                dve.wait_ge(mod_done, 4 * (9 * layer + chunk + 1))
                c = 8 * (9 * layer + chunk)
                link(dve.tensor_scalar(gate[:, :, :], mod[:, c:c + 8, :], factor, None, ALU.mult))

            def inverse(n):
                nt = norm_tok[n] // P
                dve.wait_ge(sd_done, n + 1)
                link(dve.reciprocal(rms[:, n, 0:nt], rms[:, n, 0:nt]))
                dve.tensor_tensor(scr[3][:, 0:nt * P].rearrange("p (a t) -> p a t", a=nt),
                                  ident.unsqueeze(1).broadcast_to([P, nt, P]),
                                  rms[:, n, 0:nt].unsqueeze(2).broadcast_to([P, nt, P]), ALU.mult).then_inc(diag_done, 1)

            def norm(n):
                T = norm_tok[n]
                if n > 0:
                    inverse(n)
                final = n == len(norm_tok) - 1
                dve.wait_ge(rstd_mm, n + 1)
                for kt in range(KT + AHEAD):
                    if kt < KT:
                        dve.tensor_tensor(xn[:, kt, 0:T], x[:, kt, 0:T], bank[5][:, 0:T], ALU.mult).then_inc(t_done, 1)
                    if kt >= AHEAD and not final:
                        k = kt - AHEAD
                        pool = k in POOL_KT
                        dve.wait_ge(hhi_pool if pool else hhi_act, hi_before(n, k, pool))
                        dve.tensor_tensor(h_lo[:, k, 0:T], hf[:, k, 0:T], h_hi[:, k, 0:T].bitcast(F32),
                                          ALU.subtract).then_inc(h_done, 1)

            def ffn(layer, second):
                T = tokens(layer, 2 * second)
                u = ffn_unit(layer, second)
                tile = HTILES * (2 * layer + second)
                xb = x_before(layer, 2 * second)
                for chunk, n in enumerate(CHUNKS):
                    job = paired(("pairs", layer, second, chunk))
                    jobs = planned("w2", layer, second, chunk)
                    with dve.Fori(0, n) as i:
                        if job:
                            mod_sum(job, range(KT), i)
                        lo_split(u + 2, i)
                        for t in range(2):
                            dve.wait_ge(silu_done, i * 2 + (TOKENS2 + tile + t + 1))
                            dve.tensor_tensor(scr[2 + t][:, 0:T], scr[t][:, 0:T], bank[t][:, 0:T],
                                              ALU.mult).then_inc(prod_done, 1)
                            dve.wait_ge(hhid_done, i * 2 + (tile + t + 1))
                            one = "p (a t) -> p a t"
                            dve.tensor_tensor(hid_lo[:, bass.ds(i * 2 + t, 1), 0:T],
                                              scr[2 + t][:, 0:T].rearrange(one, a=1),
                                              hid_hi[:, bass.ds(i * 2 + t, 1), 0:T].bitcast(F32),
                                              ALU.subtract).then_inc(hid_done, 1)
                        if job:
                            mod_out(job[0], 6 + job[1], i)
                        lo_split(u + 3, i)
                    u += 2 * n
                    tile += 2 * n
                    if chunk == 0:
                        prepare_gate(layer, 2 + 6 * second, 0.5)
                    for j in range(W2_UNITS):
                        for mod_job in jobs[j:j + 1]:
                            mod_sum(mod_job, range(KT))
                        update(u, j, (4, 5) if j % 2 == 0 else (2, 3), T,
                               1 + 2 * second + layer * 3 if chunk == 2 else None)
                        for mod_job in jobs[j:j + 1]:
                            mod_out(mod_job[0], 6 + mod_job[1])
                        u += 1
                    xb += KT

            def update(u, j, banks, T, n):
                for t in range(2):
                    if t == 0:
                        dve.wait_ge(half_mm, u + 1)
                    else:
                        dve.wait_ge(unit_mm[u % 2], u // 2 + 1)
                    kt = 2 * j + t
                    for c in range(T // LAT):
                        sl = slice(c * LAT, (c + 1) * LAT)
                        ins = dve.scalar_tensor_tensor(out=x[:, kt, sl], in0=bank[banks[t]][:, sl],
                                                       scalar=gate[:, kt, c:c + 1], in1=x[:, kt, sl],
                                                       op0=ALU.mult, op1=ALU.add)
                    ins.then_inc(x_done, 1)
                last = j == W2_UNITS - 1
                if not (last and n is not None) and u + 2 < UNITS:
                    lo_split(u + 2)
                if n is not None:
                    add_squares(n, [2 * j, 2 * j + 1])
                    if last and u + 2 < UNITS:
                        lo_split(u + 2)

            def mixer(layer):
                u = in_unit(layer)
                Tq = tokens(layer, 2)
                cb, pb = CHAINS * layer, PLAIN * layer
                plains = [pb]

                def chain_tok(n):
                    return TOK if n == 4 else Tq

                def head_norm(n):
                    T = chain_tok(n)
                    col = V_KN if n == 4 else V_QN
                    dve.wait_ge(qsd, cb + n + 1)
                    link(dve.reciprocal(scr[2 + n % 2][:, 0:T], scr[2 + n % 2][:, 0:T]))
                    dve.scalar_tensor_tensor(out=scr[n % 2][:, 0:T], in0=scr[n % 2][:, 0:T],
                                             scalar=vec[:, layer, col:col + 1], in1=scr[2 + n % 2][:, 0:T],
                                             op0=ALU.mult, op1=ALU.mult).then_inc(qn_done, 1)

                def rope(n):
                    q, tmp = scr[n % 2][:, 0:LAT], scr[2 + n % 2][:, 0:LAT]
                    dve.wait_ge(rot_mm, cb + n + 1)
                    dve.tensor_tensor(tmp, bank[6 + n % 2][:, 0:LAT], sinv, ALU.mult)
                    link(dve.tensor_tensor(q, q, cosv, ALU.mult))
                    dve.tensor_tensor(q, q, tmp, ALU.add).then_inc(rope_done, 1)

                def chain_lo(n):
                    T = chain_tok(n)
                    dve.wait_ge(q_hi_done, cb + n + 1)
                    hi, lo = (k_hi[:, 4, 0:T], k_lo[:, 4, 0:T]) if n == 4 else (hid_hi[:, 4 + n, 0:T], hid_lo[:, 4 + n, 0:T])
                    dve.tensor_tensor(lo, scr[n % 2][:, 0:T], hi.bitcast(F32), ALU.subtract).then_inc(qk_done, 1)

                def plain(hi, lo, src):
                    plains[0] += 1
                    dve.wait_ge(pj_hi, plains[0])
                    dve.tensor_tensor(lo, src, hi.bitcast(F32), ALU.subtract).then_inc(pj_done, 1)

                def plain_of(j, t):
                    b = 2 * (j % 2)
                    hi, src = plain_tile(j, t, hid_hi, k_hi, v_hi, b, Tq)
                    lo, _ = plain_tile(j, t, hid_lo, k_lo, v_lo, b, Tq)
                    plain(hi, lo, src)

                lo_split(u + 2)
                head_norm(0)
                head_norm(1)
                lo_split(u + 3)
                rope(0)
                rope(1)
                chain_lo(0)
                chain_lo(1)
                head_norm(2)
                head_norm(3)
                lo_split(u + 4)
                rope(2)
                rope(3)
                chain_lo(2)
                chain_lo(3)
                plain(v_hi[:, :, 512:640], v_lo[:, :, 512:640], bank[1][:, :].rearrange("p (a n) -> p a n", n=P))
                plain(hid_hi[:, 0, 0:Tq], hid_lo[:, 0, 0:Tq], bank[2][:, 0:Tq])
                head_norm(4)
                plain(hid_hi[:, 1, 0:Tq], hid_lo[:, 1, 0:Tq], bank[3][:, 0:Tq])
                lo_split(u + 5)
                rope(4)
                chain_lo(4)
                for j in range(4, IN_UNITS):
                    beside = layer == 0 and j in MODS_BESIDE_IN
                    job = planned("w_in")[MODS_BESIDE_IN.index(j)] if beside else None
                    if job:
                        mod_sum(job, range(KT))
                    plain_of(j, 0)
                    plain_of(j, 1)
                    if job:
                        mod_out(job[0], 6 + job[1])
                    lo_split(u + j + 2)

                work = items(layer)
                i0 = ITEMS0[layer]
                for i in range(len(work) + 2):
                    if i < len(work):
                        grouped, tt, hd = work[i]
                        n = i0 + i
                        N = TOK if tt < 2 else TOK - LAT
                        dve.wait_ge(s_mm, n + 1)
                        S = bank[i % 2]
                        if not grouped and tt < 2:
                            dve.wait_ge(bias_done, layer + 1)
                            link(dve.scalar_tensor_tensor(
                                out=S[:, 0:LAT].rearrange("p (a b) -> p a b", a=ROWS), in0=bias[:, tt, hd, :, ::-1],
                                scalar=1.0 / SCALE, in1=S[:, 0:LAT].rearrange("p (a b) -> p a b", a=ROWS), op0=ALU.mult, op1=ALU.add))
                        dve.tensor_scalar(S[:, 0:N], S[:, 0:N], -SCALE, None, ALU.mult, ALU.min,
                                          accum_out=nmax[:, i:i + 1]).then_inc(nm_done, 1)
                    if 1 <= i <= len(work):
                        k = i - 1
                        kk = 4 if work[k][1] < 2 else 2
                        dve.wait_ge(pthi_done, i0 + k + 1)
                        dve.tensor_tensor(pt_lo[k % 2][:, 0:kk, :],
                                          bank[2 + k % 2][:, 0:kk * P].rearrange("p (a n) -> p a n", n=P),
                                          pt_hi[k % 2][:, 0:kk, :].bitcast(F32), ALU.subtract).then_inc(ptlo_done, 1)
                    if i >= 2:
                        k = i - 2
                        grouped, tt, hd = work[k]
                        link(dve.reciprocal(linv[:, k:k + 1], lsum[:, k:k + 1]))
                        dve.wait_ge(o_mm, i0 + k + 1)
                        c = 512 * grouped + HD * hd
                        dve.tensor_scalar(o[:, tt, c:c + HD], bank[4 + k % 2][:, 0:HD], linv[:, k:k + 1], None,
                                          ALU.mult).then_inc(o_done, 1)
                tts = Tq // P
                dve.wait_ge(orstd_done, 2 * layer + 2)
                for g in range(2):
                    link(dve.reciprocal(oss[:, 4 * g:4 * g + tts], oss[:, 4 * g:4 * g + tts]))
                for g in (1, 0):
                    for tt in range(tts):
                        dve.tensor_scalar(o[:, tt, 512 * g:512 * (g + 1)], o[:, tt, 512 * g:512 * (g + 1)],
                                          oss[:, 4 * g + tt:4 * g + tt + 1], None, ALU.mult).then_inc(onorm_done, 1)
                for ct in range(KT):
                    dve.wait_ge(y_hi_done, KT * layer + ct + 1)
                    dve.scalar_tensor_tensor(out=hid_lo[:, ct, 0:Tq], in0=bank[ct % 4][:, 0:Tq],
                                             scalar=vec[:, layer, V_GO + ct:V_GO + ct + 1],
                                             in1=hid_hi[:, ct, 0:Tq].bitcast(F32),
                                             op0=ALU.mult, op1=ALU.subtract).then_inc(y_done, 1)
                prepare_gate(layer, 5, 1.0)
                uo = out_unit(layer)
                for j in range(OUT_UNITS):
                    if layer == 0:
                        mod_sum(planned("w_out")[j], range(KT))
                    update(uo + j, j, (4, 5) if j % 2 == 0 else (6, 7), Tq, 3 * layer + 2)
                    if layer == 0:
                        mod_out(planned("w_out")[j][0], j % 2)

            dve.memset(ones[:, :], 1.0)
            dve.memset(eps[:, 0:1], EPS).then_inc(ready, 1)
            dve.memset(lsum[:, :], 1.0).then_inc(silu_done, TOKENS2)
            dve.memset(nmax[:, :], 0.0).then_inc(prod_done, TOKENS2)
            dve.wait_ge(prod_done, TOKENS2)
            add_squares(0, range(KT))
            dve.wait_ge(cs_done, 1)
            for m, s, _, _ in planned("first"):
                if by_vector(m):
                    mod_sum((m, s, 0, None), range(KT))
                    mod_out(m - 1, 6)
                    mod_out(m, 7)
                if m == 1:
                    inverse(0)
            prepare(0, V_N1, 0)
            lo_split(0)
            lo_split(1)
            norm(0)
            for layer in range(DEPTH):
                ffn(layer, False)
                prepare(layer, V_NMIX, 3)
                norm(3 * layer + 1)
                mixer(layer)
                prepare(layer, V_N2, 6)
                norm(3 * layer + 2)
                ffn(layer, True)
                if layer < DEPTH - 1:
                    prepare(layer + 1, V_N1, 0)
                norm(3 * layer + 3)

        @block.gpsimd
        def _(pool):
            def norm(n):
                T = norm_tok[n]
                for kt in POOL_KT:
                    pool.wait_ge(hf_done, hf_before(n) + (T // LAT) * (kt + 1))
                    pool.tensor_copy(h_hi[:, kt, 0:T], hf[:, kt, 0:T]).then_inc(hhi_pool, 1)

            def mask(layer):
                pool.wait_ge(bias_in, 16 * ROWS * ROWS * (layer + 1))
                masks = 0
                for lo, sign, base in ((WIN_W, -1, GRID_W - 1 + WIN_W // 2), (0, 1, WIN_W // 2 - GRID_W)):
                    for qt in range(2):
                        for p0 in (0, GRID_W):
                            v = bias[p0:p0 + GRID_W, qt].rearrange("p h r c -> p (h r) c")[:, :, lo:lo + GRID_W - WIN_W]
                            pool.affine_select(out=v, in_=v, compare_op=ALU.is_ge, fill=-1e30,
                                               base=base + sign * lo,
                                               pattern=[[0, HEADS * ROWS], [sign, GRID_W - WIN_W]],
                                               channel_multiplier=sign).then_inc(g_masked, 1)
                    masks += 4
                    pool.wait_ge(g_masked, 8 * layer + masks)
                pool.memset(flag[:, :], 0.0).then_inc(bias_done, 1)

            norm(0)
            for layer in range(DEPTH):
                norm(3 * layer + 1)
                mask(layer)
                norm(3 * layer + 2)
                if layer < DEPTH - 1:
                    norm(3 * layer + 3)

        @block.tensor
        def _(pe):
            def product(out, terms, waits=None):
                n, of = terms
                for kt in range(n):
                    if waits is not None:
                        pe.wait_ge(waits[0], waits[1] + kt + 1)
                    a_hi, a_lo, b_hi, b_lo = of(kt)
                    pe.matmul(out, a_hi, b_hi, start=kt == 0, stop=False)
                    pe.matmul(out, a_hi, b_lo, start=False, stop=False)
                    mm = pe.matmul(out, a_lo, b_hi, start=False, stop=kt == n - 1)
                return mm

            def weights(s, c0, width, rhs_hi, rhs_lo, T, n=KT):
                return n, lambda kt: (whi[s][:, kt, c0:c0 + width], wlo[s][:, kt, c0:c0 + width],
                                      rhs_hi[:, kt, 0:T], rhs_lo[:, kt, 0:T])

            def mod_total(m, s, b, i=0):
                if not isinstance(i, int) or m >= 2:
                    pe.wait_ge(mod_done, m - 1 + i)
                pe.wait_ge(mod_step, i * MSTEPS + mod_steps(m + 1))
                for t in range(2):
                    for c in range(2):
                        mm = pe.matmul(bank[b][:, 2 * t + c:2 * t + c + 1], macc[s][:, c, t * P:(t + 1) * P],
                                       ones[:, 0:1], start=True, stop=True)
                mm.then_inc(mod_mm, 1)

            def mod_unit(m):
                if m >= 2:
                    pe.wait_ge(mod_done, m - 1)
                pe.wait_ge(mfirst_in[m], 16)
                for t in range(2):
                    for kt in range(KT):
                        mm = pe.matmul(bank[6 + m % 2][:, 2 * t:2 * t + 2], mfirst[m][:, kt, t * P:(t + 1) * P],
                                       cs[:, kt, :], start=kt == 0, stop=kt == KT - 1)
                mm.then_inc(mod_mm, 1)

            def stats(n):
                pe.wait_ge(acc_done, (KT - 1) * (n + 1))
                for a in range(norm_tok[n] // P):
                    mm = pe.matmul(bank[4][:, a:a + 1], scr[2][:, a * P:(a + 1) * P], ones[:, 0:1], start=True, stop=True)
                mm.then_inc(ssq_mm, 1)

            def spread(n):
                T = norm_tok[n]
                pe.wait_ge(diag_done, n + 1)
                pe.matmul(bank[5][:, 0:T], ones[:, :], scr[3][:, 0:T], start=True, stop=True).then_inc(rstd_mm, 1)

            def first_unit(banks, s, n, T):
                for kt in range(KT):
                    pe.wait_ge(h_done, KT * n + kt + 1)
                    for t in range(2):
                        out = bank[banks[t]][:, 0:T]
                        hi, lo = whi[s][:, kt, t * P:(t + 1) * P], wlo[s][:, kt, t * P:(t + 1) * P]
                        pe.matmul(out, hi, h_hi[:, kt, 0:T], start=kt == 0, stop=False)
                        pe.matmul(out, hi, h_lo[:, kt, 0:T], start=False, stop=False)
                        mm = pe.matmul(out, lo, h_hi[:, kt, 0:T], start=False, stop=kt == KT - 1)
                        if kt == KT - 1:
                            mm.then_inc(half_mm if t == 0 else unit_mm[s], 1)

            def ffn(layer, second):
                T = tokens(layer, 2 * second)
                n_norm = 3 * layer + 2 * second
                u = ffn_unit(layer, second)
                tile = HTILES * (2 * layer + second)
                xb = x_before(layer, 2 * second)
                for chunk, n in enumerate(CHUNKS):
                    job = paired(("pairs", layer, second, chunk))

                    def pair(i, first):
                        for j in range(2):
                            s = (u + j) % 2
                            pe.wait_ge(split[s], i + ((u + j) // 2 + 1))
                            if j == 1 and xb > 0:
                                pe.wait_ge(x_done, xb)
                            if j == 0 and first:
                                pe.wait_ge(prod_done, tile + 2)
                                first_unit((0, 1), s, n_norm, T)
                                continue
                            for t in range(2):
                                pe.wait_ge((prod_done, silu_done)[j], i * 2 + (tile + t + 1))
                                mm = product(bank[2 * j + t][:, 0:T], weights(s, t * P, P, h_hi, h_lo, T))
                                mm.then_inc(half_mm if t == 0 else unit_mm[s], 1)
                                if j == 1 and t == 0 and job:
                                    mod_total(job[0], job[1], 6 + job[1], i)

                    if chunk == 0:
                        pair(0, True)
                    with pe.Fori(1 if chunk == 0 else 0, n) as i:
                        pair(i, False)
                    u += 2 * n
                    for j in range(W2_UNITS):
                        s = u % 2
                        pe.wait_ge(split[s], u // 2 + 1)
                        b = 4 if j % 2 == 0 else 2
                        for t in range(2):
                            if j >= 2:
                                pe.wait_ge(x_done, xb + 2 * (j - 2) + t + 1)
                            elif j == 0 and xb > 0:
                                pe.wait_ge(x_done, xb)
                            mm = product(bank[b + t][:, 0:T], weights(s, t * P, P, hid_hi, hid_lo, T, 2 * n),
                                         (hid_done, tile) if j == 0 and t == 0 else None)
                            mm.then_inc(half_mm if t == 0 else unit_mm[s], 1)
                        for mod_job in planned("w2", layer, second, chunk)[j:j + 1]:
                            mod_total(mod_job[0], mod_job[1], 6 + mod_job[1])
                        u += 1
                    tile += 2 * n
                    xb += KT

            def mixer(layer):
                u0 = in_unit(layer)
                Tq = tokens(layer, 2)
                cb, pb = CHAINS * layer, PLAIN * layer
                xb = x_before(layer, 1)

                def tile_of(j, t):
                    u = u0 + j
                    s = u % 2
                    if t == 0:
                        pe.wait_ge(split[s], u // 2 + 1)
                    b = 2 * (j % 2) + t
                    if j == 2 and t == 0:
                        pe.wait_ge(qsq, cb + 1)
                    elif j == 2:
                        pe.wait_ge(qsq, cb + 2)
                    elif j == 3:
                        pe.wait_ge(qsq, cb + 3 + t)
                    elif j == 4 and t == 0:
                        pe.wait_ge(qsq, cb + 5)
                    elif j == 4:
                        pe.wait_ge(pj_done, pb + 1)
                    elif j >= 5:
                        pe.wait_ge(pj_done, pb + 2 * (j - 5) + t + 2)
                    if j >= 7 or (j, t) == (2, 1):
                        c0, width, tts = (P, P, range(4)) if j == 2 else (0, UW, range(2 * t, 2 * t + 2))
                        for a, tt in enumerate(tts):
                            tk = slice(tt * P, (tt + 1) * P)
                            mm = product(bank[b][:, a * width:(a + 1) * width],
                                         (KT, lambda kt: (h_hi[:, kt, tk], h_lo[:, kt, tk],
                                                          whi[s][:, kt, c0:c0 + width], wlo[s][:, kt, c0:c0 + width])))
                    else:
                        T = Tq if j < 5 and j != 2 else TOK
                        mm = product(bank[b][:, 0:T], weights(s, t * P, P, h_hi, h_lo, T))
                    mm.then_inc(half_mm if t == 0 else unit_mm[s], 1)

                def head_sums(n):
                    T = TOK if n == 4 else Tq
                    pe.wait_ge(qsq, cb + n + 1)
                    pe.matmul(bank[4 + n % 2][:, 0:T], blk, scr[2 + n % 2][:, 0:T], start=True,
                              stop=True).then_inc(qss_mm, 1)

                def rotate(n):
                    pe.wait_ge(qn_done, cb + n + 1)
                    pe.matmul(bank[6 + n % 2][:, 0:LAT], rot, scr[n % 2][:, 0:LAT], start=True,
                              stop=True).then_inc(rot_mm, 1)

                pe.wait_ge(split[u0 % 2], u0 // 2 + 1)
                pe.wait_ge(x_done, xb)
                first_unit((0, 1), u0 % 2, 3 * layer + 1, Tq)
                tile_of(1, 0)
                head_sums(0)
                head_sums(1)
                tile_of(1, 1)
                rotate(0)
                rotate(1)
                tile_of(2, 0)
                head_sums(2)
                head_sums(3)
                tile_of(2, 1)
                rotate(2)
                rotate(3)
                tile_of(3, 0)
                head_sums(4)
                tile_of(3, 1)
                rotate(4)
                for j in range(4, IN_UNITS):
                    tile_of(j, 0)
                    tile_of(j, 1)
                    if layer == 0 and j in MODS_BESIDE_IN:
                        m, s, _, _ = planned("w_in")[MODS_BESIDE_IN.index(j)]
                        mod_total(m, s, 6 + s)

                work = items(layer)
                i0 = ITEMS0[layer]
                pe.wait_ge(qk_done, cb + CHAINS)
                pe.wait_ge(pj_done, pb + PLAIN)
                for i in range(len(work) + 2):
                    if i < len(work):
                        grouped, tt, hd = work[i]
                        half = HD * (hd // 4 if grouped else hd % 2)
                        qt = 4 + hd % 4 if grouped else hd // 2
                        kt = 4 if grouped else hd // 2
                        ks = slice(0, TOK) if tt < 2 else slice(LAT, TOK)
                        N = ks.stop - ks.start
                        pp = slice(half, half + HD)
                        tk = slice(tt * P, (tt + 1) * P)
                        if i >= 2:
                            pe.wait_ge(exp_done, i0 + i - 1)
                        product(bank[i % 2][:, 0:N],
                                (1, lambda _: (hid_hi[pp, qt, tk], hid_lo[pp, qt, tk], k_hi[pp, kt, ks], k_lo[pp, kt, ks]))
                                ).then_inc(s_mm, 1)
                    if 1 <= i <= len(work):
                        k = i - 1
                        kk = 4 if work[k][1] < 2 else 2
                        pe.wait_ge(exp_done, i0 + k + 1)
                        if k >= 2:
                            pe.wait_ge(ptlo_done, i0 + k - 1)
                        for a in range(kk):
                            mm = pe.transpose(bank[2 + k % 2][:, a * P:(a + 1) * P], scr[k % 2][:, a * P:(a + 1) * P], ident)
                        mm.then_inc(t_mm, 1)
                    if i >= 2:
                        k = i - 2
                        grouped, tt, hd = work[k]
                        kk = 4 if tt < 2 else 2
                        c = 512 + HD * (hd // 4) if grouped else HD * hd
                        pe.wait_ge(ptlo_done, i0 + k + 1)
                        if k >= 2:
                            pe.wait_ge(o_done, i0 + k - 1)
                        product(bank[4 + k % 2][:, 0:HD],
                                (kk, lambda a: (pt_hi[k % 2][:, a, :], pt_lo[k % 2][:, a, :],
                                                v_hi[:, 4 - kk + a, c:c + HD], v_lo[:, 4 - kk + a, c:c + HD]))
                                ).then_inc(o_mm, 1)
                tts = Tq // P
                n_on = sum(2 * tokens(i, 2) // P for i in range(layer))
                for c in range(KT):
                    ct = (c + 4) % KT
                    ct = c
                    if c >= 4:
                        pe.wait_ge(y_done, KT * layer + c - 3)
                    pe.wait_ge(onorm_done, n_on + 2 * tts)
                    for tt in range(tts):
                        mm = pe.transpose(bank[c % 4][:, tt * P:(tt + 1) * P], o[:, tt, ct * P:(ct + 1) * P], ident)
                    mm.then_inc(yt_mm, 1)
                for j in range(OUT_UNITS):
                    u = out_unit(layer) + j
                    s = u % 2
                    pe.wait_ge(split[s], u // 2 + 1)
                    b = 4 if j % 2 == 0 else 6
                    for t in range(2):
                        if j >= 2:
                            pe.wait_ge(x_done, xb + 2 * (j - 2) + t + 1)
                        mm = product(bank[b + t][:, 0:Tq], weights(s, t * P, P, hid_hi, hid_lo, Tq),
                                     (y_done, KT * layer) if j == 0 and t == 0 else None)
                        mm.then_inc(half_mm if t == 0 else unit_mm[s], 1)
                    if layer == 0:
                        mod_total(planned("w_out")[j][0], j % 2, j % 2)

            pe.wait_ge(ready, 1)
            pe.wait_ge(cs_done, 1)
            for m, s, _, _ in planned("first"):
                if by_vector(m):
                    mod_total(m, s, 6 + m % 2)
                else:
                    mod_unit(m)
                if m == 0:
                    stats(0)
                if m == 1:
                    spread(0)
            for layer in range(DEPTH):
                ffn(layer, False)
                stats(3 * layer + 1)
                spread(3 * layer + 1)
                mixer(layer)
                stats(3 * layer + 2)
                spread(3 * layer + 2)
                ffn(layer, True)
                stats(3 * layer + 3)
                spread(3 * layer + 3)


def _constants():
    c = np.zeros((P, C_COLS), np.float32)
    r = np.arange(P)
    c[:, C_ID:C_ID + P] = np.eye(P, dtype=np.float32)
    c[:, C_BLK:C_BLK + P] = (r[:, None] // HD == r[None, :] // HD).astype(np.float32)
    for m in range(P):
        first = m % 32 < 16
        c[m + 16 if first else m - 16, C_ROT + m] = -1.0 if first else 1.0
    t = np.arange(LAT)
    inv = (np.float32(ROPE_THETA) ** (-np.arange(0, HD // 2, 2, dtype=np.float32) / np.float32(HD // 2))).astype(np.float32)
    for m in range(P):
        d = m % HD
        pos = (t // GRID_W if d < HD // 2 else t % GRID_W).astype(np.float32)
        ang = pos * inv[d % 16]
        c[m, C_COS:C_COS + LAT] = np.cos(ang)
        c[m, C_SIN:C_SIN + LAT] = np.sin(ang)
    return c


def kernel(x, c, ctx, c_ctx, w_mod, b_mod, norm_ffn1, ffn1_w13, ffn1_w2, norm_mix, w_in, na_rpb,
           gqa_q_norm, gqa_k_norm, out_norm_a, out_norm_b, w_out, norm_ffn2, ffn2_w13, ffn2_w2, norm_f):
    import concourse.bacc as bacc
    from concourse.bass_utils import run_bass_kernel_spmd

    def columns(v):
        return np.asarray(v).reshape(-1, P).T

    per_layer = []
    for i in range(DEPTH):
        cond = np.stack([columns(c), columns(c_ctx)], axis=2).reshape(P, 2 * KT)
        head = [np.concatenate([g[i], g[i]]).reshape(P, 1) for g in (np.asarray(gqa_q_norm), np.asarray(gqa_k_norm))]
        per_layer.append(np.concatenate(
            [columns(norm_ffn1[i]), columns(norm_mix[i]), columns(norm_ffn2[i]), columns(out_norm_a[i]),
             columns(out_norm_b[i]), *head, columns(norm_f), cond], axis=1))
    arrays = {
        "xT": np.asarray(x)[0].T, "ctxT": np.asarray(ctx)[0].T,
        "vecs": np.stack(per_layer, axis=1), "bmod": columns(b_mod), "consts": _constants(),
        "w_mod": w_mod, "ffn1_w13": ffn1_w13, "ffn1_w2": ffn1_w2, "w_in": w_in, "rpb": np.asarray(na_rpb)[..., ::-1],
        "w_out": w_out, "ffn2_w13": ffn2_w13, "ffn2_w2": ffn2_w2,
    }
    arrays = {n: np.ascontiguousarray(a) for n, a in arrays.items()}
    nc = bacc.Bacc("TRN2", target_bir_lowering=False, num_devices=1)
    args = [nc.dram_tensor(n, a.shape, mybir.dt.from_np(a.dtype), kind="ExternalInput").ap() for n, a in arrays.items()]
    out = nc.dram_tensor("outT", (D, LAT), F32, kind="ExternalOutput").ap()
    build(nc, *args, out)
    r = run_bass_kernel_spmd(nc, [arrays], core_ids=[0])
    return np.ascontiguousarray(r.results[0]["outT"].T).reshape(1, LAT, D)
```

```python
from contextlib import ExitStack

import numpy as np

import concourse.bass as bass
from concourse import mybir

F32 = mybir.dt.float32
F32R = mybir.dt.float32r
ACT = mybir.ActivationFunctionType
ALU = mybir.AluOpType

P = 128
D = 1024
KT = D // P
DEPTH = 2
LAT = 256
TOK = 512
HD = 64
HEADS = 8
GRID_W = 64
ROWS = LAT // GRID_W
WIN_W = 16
RPB_H, RPB_W = 15, 31
FF = 2816
N_MOD = 9
EPS = 1e-6
SCALE = HD ** -0.5
ROPE_THETA = 10000.0
UW = 256
IN_W = 2304
QB_COL = 1536

CHUNKS = (4, 4, 3)
W2_UNITS = D // UW
FFN_UNITS = 2 * sum(CHUNKS) + W2_UNITS * len(CHUNKS)
IN_UNITS = IN_W // UW
OUT_UNITS = D // UW
LAYER_UNITS = 2 * FFN_UNITS + IN_UNITS + OUT_UNITS
UNITS = DEPTH * LAYER_UNITS
HTILES = FF // P
X_PER_FFN = KT * len(CHUNKS)

MODS = DEPTH * N_MOD * D // UW
MODS_FIRST = 2 * D // UW

CHAINS = 5
PLAIN = 13

V_N1, V_NMIX, V_N2, V_GO, V_QN, V_KN, V_NF, V_C, V_COLS = 0, 8, 16, 24, 32, 33, 34, 42, 58
C_ID, C_BLK, C_ROT, C_COS, C_SIN, C_COLS = 0, 128, 256, 384, 640, 896

BANKS_FREE = 2

MODS_BESIDE_IN = (5, 6, 7)
MODS_BESIDE_W2 = ((4, 4, 2), (4, 4, 1), (4, 4, 1))


def mod_plan():
    plan, used = {}, [[], []]

    def take(place, slots):
        plan[place] = []
        for s in slots:
            m = MODS_FIRST + len(used[0]) + len(used[1])
            if m < MODS:
                plan[place].append((m, s, len(used[s]), used[s][-1] if used[s] else None))
                used[s].append(m)

    plan["first"] = [(m, m // 2 % 2, 0, None) for m in range(MODS_FIRST)]
    for layer, second in ((0, False), (0, True), (1, False)):
        if second:
            take("w_in", [j % 2 for j in MODS_BESIDE_IN])
            take("w_out", [j % 2 for j in range(W2_UNITS)])
        for chunk, n in enumerate(CHUNKS):
            if MODS - MODS_FIRST - len(used[0]) - len(used[1]) >= n:
                take(("pairs", layer, second, chunk), [1] * n)
            take(("w2", layer, second, chunk), [j % 2 for j in range(MODS_BESIDE_W2[layer * 2 + second][chunk])])
    return plan


PLAN = mod_plan()


def planned(*place):
    return PLAN.get(place[0] if len(place) == 1 else place, [])


def paired(place):
    assert len({(m - i, s, g - i) for i, (m, s, g, _) in enumerate(planned(*place))}) <= 1
    return planned(*place)[0] if planned(*place) else None


def ffn_unit(layer, second):
    return layer * LAYER_UNITS + (FFN_UNITS + IN_UNITS + OUT_UNITS if second else 0)


def in_unit(layer):
    return layer * LAYER_UNITS + FFN_UNITS


def out_unit(layer):
    return in_unit(layer) + IN_UNITS


def x_before(layer, stage):
    return layer * (2 * X_PER_FFN + KT) + (0, X_PER_FFN, X_PER_FFN + KT)[stage]


def items(layer):
    tiles = range(4) if layer < DEPTH - 1 else range(2)
    return [(g, tt, j, half) for g in (1, 0) for tt in tiles for j in range(4) for half in range(2)]


ITEMS0 = (0, len(items(0)), len(items(0)) + len(items(1)))
BLOCK = 8
T_LAG, O_LAG = 2, 4


def build(nc, xT, ctxT, vecs, bmod, consts, w_mod, w13_1, w2_1, w_in, rpb, w_out, w13_2, w2_2, outT):
    ctx = ExitStack()
    with ctx:
        def sem(name):
            return ctx.enter_context(nc.semaphore(name))

        at = [16512]

        def place(name, shape, dt, where=None):
            size = -(-4 * int(np.prod(shape[1:])) // 32) * 32
            if where is None:
                where = at[0]
                at[0] += size
            return nc.alloc_sbuf_tensor_at(name, shape, dt, offset=where)

        x = place("x", [P, KT, TOK], F32)
        h_hi_at = at[0]
        h_hi = place("h_hi", [P, KT, TOK], F32R)
        h_lo_at = at[0]
        h_lo = place("h_lo", [P, KT, TOK], F32R)
        yn = place("yn", [P, KT, TOK], F32, h_hi_at)
        pt_hi = [place(f"pt_hi{i}", [P, 2, 4, P], F32R, h_hi_at + 2 * i * 4 * TOK) for i in range(2)]
        pt_lo = [place(f"pt_lo{i}", [P, 2, 4, P], F32R, h_hi_at + (4 + 2 * i) * 4 * TOK) for i in range(2)]
        y_out = place("y_out", [P, KT, LAT], F32, h_hi_at)
        bias = place("bias", [P, 2, HEADS, ROWS, GRID_W], F32, h_lo_at)
        first_at = at[0]
        hid_hi = place("hid_hi", [P, 8, TOK], F32R)
        hid_lo = place("hid_lo", [P, 8, TOK], F32R)
        xn = place("xn", [P, KT, TOK], F32, first_at)
        y = place("y", [P, KT, TOK], F32, first_at)
        hf = place("hf", [P, KT, TOK], F32, first_at + 4 * 8 * TOK)
        k_hi = place("k_hi", [P, 5, TOK], F32R)
        k_lo = place("k_lo", [P, 5, TOK], F32R)
        v_hi = place("v_hi", [P, 4, 640], F32R)
        v_lo = place("v_lo", [P, 4, 640], F32R)
        mfirst = [place(f"mfirst{m}", [P, KT, UW], F32, first_at + m * 4 * KT * UW) for m in range(MODS_FIRST)]
        assert first_at + MODS_FIRST * 4 * KT * UW <= at[0]
        raw = [place(f"raw{s}", [P, KT, UW], F32) for s in range(2)]
        mraw = [place(f"mraw{s}", [P, KT, UW], F32) for s in range(2)]
        whi = [place(f"whi{s}", [P, KT, UW], F32R) for s in range(2)]
        wlo = [place(f"wlo{s}", [P, KT, UW], F32R) for s in range(2)]
        scr = [place(f"scr{i}", [P, TOK], F32) for i in range(6)]
        cst = place("cst", [P, C_COLS], F32)
        ones = place("ones", [P, P], F32)
        vec = place("vec", [P, DEPTH, V_COLS], F32)
        bm = place("bm", [P, DEPTH * 72], F32)
        mod = place("mod", [P, DEPTH * 72, 2], F32)
        cs = place("cs", [P, KT, 2], F32)
        amul = place("amul", [P, KT, 2], F32)
        gate = place("gate", [P, KT, 2], F32)
        macc = [place(f"macc{s}", [P, 2, UW], F32) for s in range(2)]
        eps = place("eps", [P, 1], F32)
        rms = place("rms", [P, 12, 4], F32)
        warm = place("warm", [P, 32], F32)
        nmax = place("nmax", [P, 64], F32)
        lsum = place("lsum", [P, 64], F32)
        linv = place("linv", [P, 64], F32)
        flag = place("flag", [P, 1], F32)
        assert at[0] <= nc.sbuf_usable_end, at[0]

        ident = cst[:, C_ID:C_ID + P]
        blk = cst[:, C_BLK:C_BLK + P]
        rot = cst[:, C_ROT:C_ROT + P]
        cosv = cst[:, C_COS:C_COS + LAT]
        sinv = cst[:, C_SIN:C_SIN + LAT]

        bank = [ctx.enter_context(nc.psum_tensor(f"bank{b}", [P, TOK], F32)) for b in range(8)]

        more_in = sem("more_in")
        const_in, x_in, bias_in, stored = sem("const_in"), sem("x_in"), sem("bias_in"), sem("stored")
        raw_in = [sem(f"raw_in{s}") for s in range(2)]
        w_hi = [sem(f"w_hi{s}") for s in range(2)]
        split = [sem(f"split{s}") for s in range(2)]
        half_mm = sem("half_mm")
        unit_mm = [sem(f"unit_mm{s}") for s in range(2)]
        mfirst_in = [sem(f"mfirst_in{m}") for m in range(MODS_FIRST)]
        mod_in = [sem(f"mod_in{s}") for s in range(2)]
        mod_step, mod_mm, mod_done = sem("mod_step"), sem("mod_mm"), sem("mod_done")
        ready, cs_done, dchain = sem("ready"), sem("cs_done"), sem("dchain")
        silu_done, prod_done, hhid_done, hid_done = (
            sem(n) for n in ("silu_done", "prod_done", "hhid_done", "hid_done"))
        x_done, sq_done, acc_done, ssq_mm, sd_done = (
            sem(n) for n in ("x_done", "sq_done", "acc_done", "ssq_mm", "sd_done"))
        t_done, hf_done, hhi_act, hhi_pool, h_done = (
            sem(n) for n in ("t_done", "hf_done", "hhi_act", "hhi_pool", "h_done"))
        diag_done, rstd_mm, hf0_done = sem("diag_done"), sem("rstd_mm"), sem("hf0_done")
        qsq, qss_mm, qsd, qn_done, rot_mm, rope_done, q_hi_done, qk_done = (
            sem(n) for n in ("qsq", "qss_mm", "qsd", "qn_done", "rot_mm", "rope_done", "q_hi_done", "qk_done"))
        pj_hi, pj_done = sem("pj_hi"), sem("pj_done")
        bias_done, s_mm, nm_done, exp_done = (sem(n) for n in ("bias_done", "s_mm", "nm_done", "exp_done"))
        linv_done, pdiag_done, t_mm, pthi_done, ptlo_done, o_mm, y_out_done = (
            sem(n) for n in ("linv_done", "pdiag_done", "t_mm", "pthi_done", "ptlo_done", "o_mm", "y_out_done"))
        ysq_done, ysum_done, yss_mm, yrms_done, ydiag_done, yrstd_mm, yn_done, y_hi_done, y_done = (
            sem(n) for n in ("ysq_done", "ysum_done", "yss_mm", "yrms_done", "ydiag_done", "yrstd_mm", "yn_done",
                             "y_hi_done", "y_done"))
        f_done, g_masked = sem("f_done"), sem("g_masked")

        def tokens(layer, stage):
            return TOK if layer < DEPTH - 1 or stage < 2 else LAT

        norm_tok = [TOK] * 5 + [LAT] * 2

        def unit_after_norm(n):
            layer, stage = divmod(n, 3)
            return (ffn_unit(layer, False), in_unit(layer), ffn_unit(layer, True))[stage]

        POOL_KT = (2, 5)
        H_ORDER = (0, 1, 3, 2, 4, 6, 5, 7)
        NORM_STEPS = list(zip("xxlxxlxlxlxlxlll", (0, 1, 0, 2, 3, 1, 4, 3, 5, 2, 6, 4, 7, 6, 5, 7)))
        AHEAD = 3

        def hi_before(n, k, pool):
            mine = [j for j in range(KT) if (j in POOL_KT) == pool]
            return n * len(mine) + sum(j <= k for j in mine)

        def hf_before(n):
            return sum((KT - 1) * norm_tok[k] // LAT for k in range(n))

        MSTEPS = 2 * KT

        def by_vector(m):
            return m >= MODS_FIRST or m % 2 == 1

        FIRST_ORDER = (0, 2, 1, 4, 3, 6, 5, 7)

        def mod_steps(m):
            return MSTEPS * sum(by_vector(k) for k in range(m))

        def arrivals(u):
            extra = {in_unit(i) + j: 3 for i in range(DEPTH) for j in range(2)}
            extra.update({out_unit(i) + j: 2 for i in range(DEPTH) for j in range(OUT_UNITS)})
            return 16 * (u // 2 + 1 + sum(n for k, n in extra.items() if k <= u and k % 2 == u % 2))

        Y_ORDER = (4, 5, 6, 7, 0, 1, 2, 3)

        def blocks_before(layer):
            return ITEMS0[layer] // BLOCK

        def plain_tile(j, t, q_dst, k_dst, v_dst, b, Tq):
            if j < 5:
                return q_dst[:, 2 * (j - 3) + t, 0:Tq], bank[b + t][:, 0:Tq]
            if j < 7:
                return k_dst[:, 2 * (j - 5) + t, :], bank[b + t][:, :]
            c = (j - 7) * UW
            return v_dst[:, 2 * t:2 * t + 2, c:c + UW], bank[b + t][:, :].rearrange("p (a n) -> p a n", n=UW)

        block = ctx.enter_context(nc.Block())

        @block.sync
        def _(sp):
            mod_v = [w_mod[i].rearrange("(k p) n -> p k n", p=P) for i in range(DEPTH)]

            def load_first(ms):
                for m in ms:
                    sp.dma_start(mfirst[m][:, :, :], mod_v[0][:, :, m * UW:(m + 1) * UW]).then_inc(mfirst_in[m], 16)

            sp.dma_start(vec[:, :, :], vecs).then_inc(const_in, 16)
            load_first(range(2))
            sp.dma_start(x[:, :, 0:LAT], xT.rearrange("(k p) t -> p k t", p=P)).then_inc(x_in, 16)
            sp.dma_start(x[:, :, LAT:TOK], ctxT.rearrange("(k p) t -> p k t", p=P)).then_inc(x_in, 16)
            sp.dma_start(bm[:, :], bmod).then_inc(more_in, 16)
            sp.dma_start(cst[:, :], consts).then_inc(more_in, 16)
            load_first(range(2, 6))
            w13_first = w13_1[0].rearrange("(k p) n -> p k n", p=P)
            sp.dma_start(raw[0][:, :, :], w13_first[:, :, 0:UW]).then_inc(raw_in[0], 16)
            load_first(range(6, MODS_FIRST))
            sp.dma_start(raw[1][:, :, :], w13_first[:, :, FF:FF + UW]).then_inc(raw_in[1], 16)

            def load_unit(slot, gen, src):
                if not isinstance(gen, int) or gen > 0:
                    sp.wait_ge(split[slot], gen)
                sp.dma_start(raw[slot][:, 0:src.shape[1], :], src).then_inc(raw_in[slot], 16)

            def load_mod(job, i=0):
                m, s, _, prev = job
                if not isinstance(i, int):
                    sp.wait_ge(mod_step, i * MSTEPS + mod_steps(m))
                elif prev is not None:
                    sp.wait_ge(mod_step, mod_steps(prev + 1))
                lay, c = divmod(m * UW, N_MOD * D)
                cols = slice(c, c + UW) if isinstance(i, int) else bass.ds(i * UW + c, UW)
                sp.dma_start(mraw[s][:, :, :], mod_v[lay][:, :, cols]).then_inc(mod_in[s], 16)

            def ffn(layer, second):
                w13 = (w13_2 if second else w13_1)[layer].rearrange("(k p) n -> p k n", p=P)
                w2 = (w2_2 if second else w2_1)[layer].rearrange("(k p) n -> p k n", p=P)
                u = ffn_unit(layer, second)
                pair = 0
                for chunk, n in enumerate(CHUNKS):
                    job = paired(("pairs", layer, second, chunk))

                    def pair_loads(i):
                        for j, base in enumerate((0, FF)):
                            c = base + pair * UW
                            load_unit((u + j) % 2, i + (u + j) // 2, w13[:, :, bass.ds(i * UW + c, UW)])
                        if job:
                            load_mod(job, i)

                    if u == 0:
                        load_mod(job, 0)
                    with sp.Fori(1 if u == 0 else 0, n) as i:
                        pair_loads(i)
                    u += 2 * n
                    for j in range(W2_UNITS):
                        load_unit(u % 2, u // 2, w2[:, 2 * pair:2 * pair + 2 * n, j * UW:(j + 1) * UW])
                        for mod_job in planned("w2", layer, second, chunk)[j:j + 1]:
                            load_mod(mod_job)
                        u += 1
                    pair += n

            def mixer(layer):
                win = w_in[layer].rearrange("(k p) n -> p k n", p=P)
                u = in_unit(layer)
                for j in range(2):
                    s = u % 2
                    if u >= 2:
                        sp.wait_ge(split[s], u // 2)
                    for t in range(2):
                        for g in range(2):
                            c = QB_COL + HD * (2 * j + t + 4 * g)
                            to = t * P + g * HD
                            sp.dma_start(raw[s][:, :, to:to + HD], win[:, :, c:c + HD]).then_inc(raw_in[s], 16)
                    u += 1
                for j, c in enumerate((2048, 0, 256, 512, 768, 1024, 1280), 2):
                    load_unit(u % 2, u // 2, win[:, :, c:c + UW])
                    if layer == 0 and j in MODS_BESIDE_IN:
                        load_mod(planned("w_in")[MODS_BESIDE_IN.index(j)])
                    u += 1
                last = in_unit(layer) + IN_UNITS - 1
                wo = w_out[layer].rearrange("(k p) n -> p k n", p=P)
                wb = w_out[layer][HEADS * HD:].rearrange("(g j p) n -> g p j n", g=2, p=HD)

                def out_loads(js):
                    for j in js:
                        uo = out_unit(layer) + j
                        c = slice(j * UW, (j + 1) * UW)
                        load_unit(uo % 2, uo // 2, wo[:, 0:4, c])
                        for g in range(2):
                            rows = raw[uo % 2][g * HD:(g + 1) * HD, 4:8, :]
                            sp.dma_start(rows, wb[g][:, :, c]).then_inc(raw_in[uo % 2], 16)
                        if layer == 0:
                            load_mod(planned("w_out")[j])

                out_loads(range(2))
                sp.wait_ge(unit_mm[last % 2], last // 2 + 1)
                for qr in range(ROWS):
                    for kr in range(ROWS):
                        src = bass.AP(tensor=rpb.tensor,
                                      offset=layer * HEADS * RPB_H * RPB_W + (kr - qr + 7) * RPB_W - (GRID_W - WIN_W),
                                      ap=[[1, GRID_W], [RPB_H * RPB_W, HEADS], [1, GRID_W]])
                        p0 = GRID_W * (qr % 2)
                        sp.dma_start(bias[p0:p0 + GRID_W, qr // 2, :, kr, :], src).then_inc(bias_in, 16)
                out_loads(range(2, OUT_UNITS))

            for layer in range(DEPTH):
                ffn(layer, False)
                mixer(layer)
                ffn(layer, True)
            sp.wait_ge(f_done, KT)
            sp.dma_start(outT.rearrange("(k p) t -> p k t", p=P), y_out[:, :, :]).then_inc(stored, 16)
            sp.wait_ge(stored, 16)

        @block.scalar
        def _(act):
            def hi_split(u, i=0):
                s = u % 2
                if u >= 2:
                    act.wait_ge(unit_mm[s], u // 2 + i)
                act.wait_ge(raw_in[s], arrivals(u) + i * 16)
                act.activation(whi[s][:, :, :], raw[s][:, :, :], ACT.Copy).then_inc(w_hi[s], 1)

            def squares(n, kts):
                T = norm_tok[n]
                for kt in kts:
                    if kt >= 3:
                        act.wait_ge(acc_done, (KT - 1) * n + kt - 2)
                    dst = scr[2] if kt == 0 else scr[kt % 2]
                    act.activation(dst[:, 0:T], x[:, kt, 0:T], ACT.Square).then_inc(sq_done, 1)

            def root(n):
                nt = norm_tok[n] // P
                act.wait_ge(ssq_mm, n + 1)
                act.activation(rms[:, n, 0:nt], bank[4][:, 0:nt], ACT.Sqrt, bias=eps[:, 0:1],
                               scale=1.0 / D).then_inc(sd_done, 1)

            warmed = [0]

            def load_table(func):
                act.activation(warm[:, warmed[0]:warmed[0] + 1], eps[:, 0:1], func)
                warmed[0] += 1

            def norm(n, shift):
                T = norm_tok[n]
                if 0 < n < len(norm_tok) - 1:
                    hi_split(unit_after_norm(n) + 1)
                if n > 0:
                    root(n)
                for kt in range(KT):
                    act.wait_ge(t_done, KT * n + kt + 1)
                    if n == len(norm_tok) - 1:
                        g = vec[:, 0, V_NF + kt:V_NF + kt + 1]
                        act.activation(y_out[:, kt, :], xn[:, kt, 0:T], ACT.Copy, scale=g).then_inc(f_done, 1)
                        continue
                    for c in range(T // LAT):
                        sl = slice(c * LAT, (c + 1) * LAT)
                        dst, done = (h_hi, hhi_act) if kt == 0 else (hf, hf_done)
                        ins = act.activation(dst[:, kt, sl], xn[:, kt, sl], ACT.Identity, scale=amul[:, kt, c:c + 1],
                                             bias=mod[:, 8 * shift + kt, c:c + 1])
                        if kt > 0 or c == T // LAT - 1:
                            ins.then_inc(done, 1)
                    if kt > 0 and kt not in POOL_KT:
                        act.wait_ge(hf_done, hf_before(n) + (T // LAT) * kt)
                        act.activation(h_hi[:, kt, 0:T], hf[:, kt, 0:T], ACT.Copy).then_inc(hhi_act, 1)

            def ffn(layer, second):
                T = tokens(layer, 2 * second)
                u = ffn_unit(layer, second)
                tile = HTILES * (2 * layer + second)
                xb = x_before(layer, 2 * second)
                for chunk, n in enumerate(CHUNKS):
                    with act.Fori(0, n) as i:
                        hi_split(u + 2, i)
                        for t in range(2):
                            if t == 0:
                                act.wait_ge(half_mm, i * 2 + (u + 2))
                            else:
                                act.wait_ge(unit_mm[(u + 1) % 2], i + ((u + 1) // 2 + 1))
                            act.activation(scr[t][:, 0:T], bank[2 + t][:, 0:T], ACT.Silu).then_inc(silu_done, 1)
                            act.wait_ge(prod_done, i * 2 + (BANKS_FREE + tile + t + 1))
                            act.activation(hid_hi[:, bass.ds(i * 2 + t, 1), 0:T],
                                           scr[2 + t][:, 0:T].rearrange("p (a t) -> p a t", a=1),
                                           ACT.Copy).then_inc(hhid_done, 1)
                        hi_split(u + 3, i)
                    u += 2 * n
                    tile += 2 * n
                    if chunk == len(CHUNKS) - 1:
                        load_table(ACT.Sqrt)
                    for j in range(W2_UNITS):
                        update(u, j, xb, layer, 1 + 2 * second + layer * 3 if chunk == 2 else None)
                        u += 1
                    xb += KT

            def update(u, j, xb, layer, n):
                last = j == W2_UNITS - 1
                if not (last and n is not None) and u + 2 < UNITS:
                    hi_split(u + 2)
                if n is not None:
                    for t in range(2):
                        act.wait_ge(x_done, xb + 2 * j + t + 1)
                        squares(n, [2 * j + t])

            def mixer(layer):
                u = in_unit(layer)
                Tq = tokens(layer, 2)
                cb, pb = CHAINS * layer, PLAIN * layer

                def chain_tok(n):
                    return TOK if n == 4 else Tq

                def q_of(n):
                    return scr[(0, 1, 4)[n % 3]]

                def s_of(n):
                    return scr[(2, 3, 5)[n % 3]]

                def take(n):
                    T = chain_tok(n)
                    b = (0, 1, 2, 3, 0)[n]
                    if n >= 3:
                        act.wait_ge(qk_done, cb + n - 2)
                    uu = u + (0, 0, 1, 1, 2)[n]
                    if n % 2 == 0:
                        act.wait_ge(half_mm, uu + 1)
                    else:
                        act.wait_ge(unit_mm[uu % 2], uu // 2 + 1)
                    act.activation(q_of(n)[:, 0:T], bank[b][:, 0:T], ACT.Copy)
                    act.activation(s_of(n)[:, 0:T], bank[b][:, 0:T], ACT.Square).then_inc(qsq, 1)

                def deviation(n):
                    T = chain_tok(n)
                    act.wait_ge(qss_mm, cb + n + 1)
                    act.activation(s_of(n)[:, 0:T], bank[4 + n % 2][:, 0:T], ACT.Sqrt,
                                   bias=eps[:, 0:1], scale=1.0 / HD).then_inc(qsd, 1)

                def chain_hi(n):
                    T = chain_tok(n)
                    act.wait_ge(rope_done, cb + n + 1)
                    dst = k_hi[:, 4, 0:T] if n == 4 else hid_hi[:, 4 + n, 0:T]
                    act.activation(dst, q_of(n)[:, 0:T], ACT.Copy).then_inc(q_hi_done, 1)

                def plain(j, t, dst, src):
                    if t == 0:
                        act.wait_ge(half_mm, u + j + 1)
                    else:
                        act.wait_ge(unit_mm[(u + j) % 2], (u + j) // 2 + 1)
                    act.activation(dst, src, ACT.Copy).then_inc(pj_hi, 1)

                take(0)
                take(1)
                hi_split(u + 2)
                deviation(0)
                deviation(1)
                take(2)
                hi_split(u + 3)
                deviation(2)
                chain_hi(0)
                chain_hi(1)
                take(3)
                take(4)
                hi_split(u + 4)
                plain(2, 1, v_hi[:, :, 512:640], bank[1][:, :].rearrange("p (a n) -> p a n", n=P))
                deviation(3)
                plain(3, 0, hid_hi[:, 0, 0:Tq], bank[2][:, 0:Tq])
                chain_hi(2)
                deviation(4)
                plain(3, 1, hid_hi[:, 1, 0:Tq], bank[3][:, 0:Tq])
                hi_split(u + 5)
                chain_hi(3)
                chain_hi(4)
                for j in range(4, IN_UNITS):
                    b = 2 * (j % 2)
                    for t in range(2):
                        plain(j, t, *plain_tile(j, t, hid_hi, k_hi, v_hi, b, Tq))
                    hi_split(u + j + 2)
                load_table(ACT.Exp)

                work = items(layer)
                i0 = ITEMS0[layer]
                b0 = blocks_before(layer)
                for i in range(len(work) + O_LAG + 3):
                    if 1 <= i <= len(work):
                        k = i - 1
                        act.wait_ge(linv_done, i0 + k + 1)
                        if k >= 3:
                            act.wait_ge(t_mm, i0 + k - 2)
                        act.activation(scr[3][:, k % 3 * P:(k % 3 + 1) * P], ident, ACT.Copy,
                                       scale=linv[:, k:k + 1]).then_inc(pdiag_done, 1)
                    if T_LAG <= i < len(work) + T_LAG:
                        k = i - T_LAG
                        kk = 4 if work[k][1] < 2 else 2
                        act.wait_ge(t_mm, i0 + k + 1)
                        if k >= 4:
                            act.wait_ge(o_mm, (i0 + k) // 2 - 1)
                        act.activation(pt_hi[k // 2 % 2][:, k % 2, 0:kk, :],
                                       bank[3 + k % 3][:, 0:kk * P].rearrange("p (a n) -> p a n", n=P),
                                       ACT.Copy).then_inc(pthi_done, 1)
                    if i < len(work):
                        N = TOK if work[i][1] < 2 else TOK - LAT
                        act.wait_ge(nm_done, i0 + i + 1)
                        if i >= 3:
                            act.wait_ge(t_mm, i0 + i - 2)
                        act.activation(scr[i % 3][:, 0:N], bank[i % 3][:, 0:N], ACT.Exp,
                                       bias=nmax[:, i:i + 1], scale=-1.0,
                                       accum_out=lsum[:, i:i + 1]).then_inc(exp_done, 1)
                    if i == len(work) + T_LAG - 1:
                        load_table(ACT.Sqrt)
                    k = i - O_LAG
                    if 0 <= k < len(work) and k % 2 == 1:
                        g, tt, j, _ = work[k]
                        act.wait_ge(o_mm, (i0 + k + 1) // 2)
                        for half in range(2):
                            pp = slice(half * HD, (half + 1) * HD)
                            act.activation(y[pp, 4 * g + j, tt * P:(tt + 1) * P],
                                           bank[6 + k // 2 % 2][pp, half * P:(half + 1) * P],
                                           ACT.Copy).then_inc(y_out_done, 1)
                    if k >= BLOCK and k % BLOCK == 0:
                        b = k // BLOCK - 1
                        g, tt = work[k - 1][:2]
                        act.wait_ge(y_out_done, i0 + k)
                        if b >= 1:
                            act.wait_ge(ysum_done, b0 + b)
                        act.activation(scr[4][:, :].rearrange("p (a t) -> p a t", a=4),
                                       y[:, 4 * g:4 * g + 4, tt * P:(tt + 1) * P], ACT.Square).then_inc(ysq_done, 1)

                tts = Tq // P
                act.wait_ge(yss_mm, b0 + 2 * tts)
                act.activation(rms[:, 7 + 2 * layer:9 + 2 * layer, 0:tts],
                               bank[7][:, 256:264].rearrange("p (g t) -> p g t", g=2)[:, :, 0:tts],
                               ACT.Sqrt, bias=eps[:, 0:1], scale=1.0 / (HEADS * HD)).then_inc(yrms_done, 1)
                for n, ct in enumerate(Y_ORDER):
                    act.wait_ge(yn_done, KT * layer + n + 1)
                    act.activation(hid_hi[:, ct, 0:Tq], yn[:, ct, 0:Tq], ACT.Copy,
                                   scale=vec[:, layer, V_GO + ct:V_GO + ct + 1]).then_inc(y_hi_done, 1)
                uo = out_unit(layer)
                xb = x_before(layer, 1)
                for j in range(OUT_UNITS):
                    update(uo + j, j, xb, layer, 3 * layer + 2)

            act.wait_ge(const_in, 16)
            act.activation(cs[:, :, :], vec[:, 0, V_C:V_C + 16].rearrange("p (k c) -> p k c", c=2),
                           ACT.Silu).then_inc(cs_done, 1)
            act.wait_ge(x_in, 32)
            squares(0, range(KT))
            act.wait_ge(ready, 1)
            root(0)
            hi_split(0)
            hi_split(1)
            norm(0, 0)
            for layer in range(DEPTH):
                load_table(ACT.Silu)
                ffn(layer, False)
                norm(3 * layer + 1, 9 * layer + 3)
                mixer(layer)
                norm(3 * layer + 2, 9 * layer + 6)
                load_table(ACT.Silu)
                ffn(layer, True)
                norm(3 * layer + 3, 9 * (layer + 1))

        @block.vector
        def _(dve):
            links = [0]

            def link(ins):
                links[0] += 1
                ins.then_inc(dchain, 1)
                dve.wait_ge(dchain, links[0])

            def lo_split(u, i=0):
                s = u % 2
                dve.wait_ge(w_hi[s], u // 2 + 1 + i)
                dve.tensor_tensor(wlo[s][:, :, :], raw[s][:, :, :], whi[s][:, :, :].bitcast(F32),
                                  ALU.subtract).then_inc(split[s], 1)

            def add_squares(n, kts):
                T = norm_tok[n]
                for kt in kts:
                    if kt == 0:
                        continue
                    dve.wait_ge(sq_done, KT * n + kt + 1)
                    if kt >= 2:
                        dve.wait_ge(acc_done, (KT - 1) * n + kt - 1)
                    dve.tensor_tensor(scr[2][:, 0:T], scr[2][:, 0:T], scr[kt % 2][:, 0:T],
                                      ALU.add).then_inc(acc_done, 1)

            def mod_sum(job, kts, i=0):
                m, s, g, prev = job
                src = mfirst[m] if m < MODS_FIRST else mraw[s]
                for kt in kts:
                    if kt == 0:
                        if m < MODS_FIRST:
                            dve.wait_ge(mfirst_in[m], 16)
                        else:
                            dve.wait_ge(mod_in[s], i * 16 + 16 * (g + 1))
                        if not isinstance(i, int):
                            dve.wait_ge(mod_mm, i + m)
                        elif m >= 4:
                            dve.wait_ge(mod_mm, FIRST_ORDER.index(m - 4) + 1 if m < MODS_FIRST else
                                        MODS_FIRST if prev is None else prev + 1)
                    for c in range(2):
                        if kt == 0:
                            dve.tensor_scalar(macc[s][:, c, :], src[:, kt, :], cs[:, kt, c:c + 1], None,
                                              ALU.mult).then_inc(mod_step, 1)
                            continue
                        dve.wait_ge(mod_step, i * MSTEPS + (mod_steps(m) + 2 * kt + c - 1))
                        dve.scalar_tensor_tensor(out=macc[s][:, c, :], in0=src[:, kt, :], scalar=cs[:, kt, c:c + 1],
                                                 in1=macc[s][:, c, :], op0=ALU.mult, op1=ALU.add).then_inc(mod_step, 1)

            def mod_out(m, b, i=0):
                dve.wait_ge(mod_mm, m + 1 + i)
                a = i * 2 + 2 * m
                cols = slice(a, a + 2) if isinstance(i, int) else bass.ds(a, 2)
                dve.tensor_tensor(mod[:, cols, :], bank[b][:, 0:4].rearrange("p (a c) -> p a c", c=2),
                                  bm[:, cols].unsqueeze(2).broadcast_to([P, 2, 2]), ALU.add).then_inc(mod_done, 1)

            def prepare(layer, col, chunk):
                dve.wait_ge(mod_done, min(MODS, 4 * (9 * layer + chunk + 2)))
                c = 8 * (9 * layer + chunk + 1)
                link(dve.scalar_tensor_tensor(
                    out=amul[:, :, :], in0=mod[:, c:c + 8, :], scalar=1.0,
                    in1=vec[:, layer, col:col + 8].unsqueeze(2).broadcast_to([P, 8, 2]),
                    op0=ALU.add, op1=ALU.mult))

            def prepare_gate(layer, chunk, factor):
                dve.wait_ge(mod_done, 4 * (9 * layer + chunk + 1))
                c = 8 * (9 * layer + chunk)
                link(dve.tensor_scalar(gate[:, :, :], mod[:, c:c + 8, :], factor, None, ALU.mult))

            def inverse(n):
                nt = norm_tok[n] // P
                dve.wait_ge(sd_done, n + 1)
                link(dve.reciprocal(rms[:, n, 0:nt], rms[:, n, 0:nt]))
                dve.tensor_tensor(scr[3][:, 0:nt * P].rearrange("p (a t) -> p a t", a=nt),
                                  ident.unsqueeze(1).broadcast_to([P, nt, P]),
                                  rms[:, n, 0:nt].unsqueeze(2).broadcast_to([P, nt, P]), ALU.mult).then_inc(diag_done, 1)

            def norm(n, shift):
                T = norm_tok[n]
                if n > 0:
                    inverse(n)
                final = n == len(norm_tok) - 1
                if n > 0 and not final:
                    lo_split(unit_after_norm(n) + 1)
                dve.wait_ge(rstd_mm, n + 1)
                for what, k in NORM_STEPS:
                    if what == "x":
                        dve.tensor_tensor(xn[:, k, 0:T], x[:, k, 0:T], bank[5][:, 0:T], ALU.mult).then_inc(t_done, 1)
                        if k == 0 and not final:
                            dve.wait_ge(t_done, KT * n + 1)
                            for c in range(T // LAT):
                                sl = slice(c * LAT, (c + 1) * LAT)
                                ins = dve.tensor_scalar(hf[:, 0, sl], xn[:, 0, sl], amul[:, 0, c:c + 1],
                                                        mod[:, 8 * shift, c:c + 1], ALU.mult, ALU.add)
                            ins.then_inc(hf0_done, 1)
                    elif not final:
                        pool = k in POOL_KT
                        if k == 0:
                            dve.wait_ge(hf0_done, n + 1)
                        dve.wait_ge(hhi_pool if pool else hhi_act, hi_before(n, k, pool))
                        dve.tensor_tensor(h_lo[:, k, 0:T], hf[:, k, 0:T], h_hi[:, k, 0:T].bitcast(F32),
                                          ALU.subtract).then_inc(h_done, 1)

            def ffn(layer, second):
                T = tokens(layer, 2 * second)
                u = ffn_unit(layer, second)
                tile = HTILES * (2 * layer + second)
                xb = x_before(layer, 2 * second)
                for chunk, n in enumerate(CHUNKS):
                    job = paired(("pairs", layer, second, chunk))
                    jobs = planned("w2", layer, second, chunk)
                    with dve.Fori(0, n) as i:
                        if job:
                            mod_sum(job, range(KT), i)
                        lo_split(u + 2, i)
                        for t in range(2):
                            dve.wait_ge(silu_done, i * 2 + (BANKS_FREE + tile + t + 1))
                            dve.tensor_tensor(scr[2 + t][:, 0:T], scr[t][:, 0:T], bank[t][:, 0:T],
                                              ALU.mult).then_inc(prod_done, 1)
                            dve.wait_ge(hhid_done, i * 2 + (tile + t + 1))
                            one = "p (a t) -> p a t"
                            dve.tensor_tensor(hid_lo[:, bass.ds(i * 2 + t, 1), 0:T],
                                              scr[2 + t][:, 0:T].rearrange(one, a=1),
                                              hid_hi[:, bass.ds(i * 2 + t, 1), 0:T].bitcast(F32),
                                              ALU.subtract).then_inc(hid_done, 1)
                        if job:
                            mod_out(job[0], 6 + job[1], i)
                        lo_split(u + 3, i)
                    u += 2 * n
                    tile += 2 * n
                    if chunk == 0:
                        prepare_gate(layer, 2 + 6 * second, 0.5)
                    for j in range(W2_UNITS):
                        for mod_job in jobs[j:j + 1]:
                            mod_sum(mod_job, range(KT))
                        update(u, j, (4, 5) if j % 2 == 0 else (2, 3), T,
                               1 + 2 * second + layer * 3 if chunk == 2 else None)
                        for mod_job in (jobs[j - 1:j] if j > 0 else []) + (jobs[j:] if j == W2_UNITS - 1 else []):
                            mod_out(mod_job[0], 6 + mod_job[1])
                        u += 1
                    xb += KT

            def update(u, j, banks, T, n):
                for t in range(2):
                    if t == 0:
                        dve.wait_ge(half_mm, u + 1)
                    else:
                        dve.wait_ge(unit_mm[u % 2], u // 2 + 1)
                    kt = 2 * j + t
                    for c in range(T // LAT):
                        sl = slice(c * LAT, (c + 1) * LAT)
                        ins = dve.scalar_tensor_tensor(out=x[:, kt, sl], in0=bank[banks[t]][:, sl],
                                                       scalar=gate[:, kt, c:c + 1], in1=x[:, kt, sl],
                                                       op0=ALU.mult, op1=ALU.add)
                    ins.then_inc(x_done, 1)
                last = j == W2_UNITS - 1
                if not (last and n is not None) and u + 2 < UNITS:
                    lo_split(u + 2)
                if n is not None:
                    add_squares(n, [2 * j, 2 * j + 1])

            def mixer(layer):
                u = in_unit(layer)
                Tq = tokens(layer, 2)
                cb, pb = CHAINS * layer, PLAIN * layer
                plains = [pb]

                def chain_tok(n):
                    return TOK if n == 4 else Tq

                def q_of(n):
                    return scr[(0, 1, 4)[n % 3]]

                def s_of(n):
                    return scr[(2, 3, 5)[n % 3]]

                def head_norm(n):
                    T = chain_tok(n)
                    col = V_KN if n == 4 else V_QN
                    dve.wait_ge(qsd, cb + n + 1)
                    link(dve.reciprocal(s_of(n)[:, 0:T], s_of(n)[:, 0:T]))
                    dve.scalar_tensor_tensor(out=q_of(n)[:, 0:T], in0=q_of(n)[:, 0:T],
                                             scalar=vec[:, layer, col:col + 1], in1=s_of(n)[:, 0:T],
                                             op0=ALU.mult, op1=ALU.mult).then_inc(qn_done, 1)

                def rope(n):
                    q, tmp = q_of(n)[:, 0:LAT], s_of(n)[:, 0:LAT]
                    dve.wait_ge(rot_mm, cb + n + 1)
                    dve.tensor_tensor(tmp, bank[6 + n % 2][:, 0:LAT], sinv, ALU.mult)
                    link(dve.tensor_tensor(q, q, cosv, ALU.mult))
                    dve.tensor_tensor(q, q, tmp, ALU.add).then_inc(rope_done, 1)

                def chain_lo(n):
                    T = chain_tok(n)
                    dve.wait_ge(q_hi_done, cb + n + 1)
                    tile = (slice(None), 4 if n == 4 else 4 + n, slice(0, T))
                    hi, lo = (k_hi[tile], k_lo[tile]) if n == 4 else (hid_hi[tile], hid_lo[tile])
                    dve.tensor_tensor(lo, q_of(n)[:, 0:T], hi.bitcast(F32), ALU.subtract).then_inc(qk_done, 1)

                def plain(hi, lo, src):
                    plains[0] += 1
                    dve.wait_ge(pj_hi, plains[0])
                    dve.tensor_tensor(lo, src, hi.bitcast(F32), ALU.subtract).then_inc(pj_done, 1)

                def plain_of(j, t):
                    b = 2 * (j % 2)
                    hi, src = plain_tile(j, t, hid_hi, k_hi, v_hi, b, Tq)
                    lo, _ = plain_tile(j, t, hid_lo, k_lo, v_lo, b, Tq)
                    plain(hi, lo, src)

                lo_split(u + 2)
                head_norm(0)
                head_norm(1)
                lo_split(u + 3)
                rope(0)
                rope(1)
                chain_lo(0)
                chain_lo(1)
                head_norm(2)
                lo_split(u + 4)
                head_norm(3)
                plain(v_hi[:, :, 512:640], v_lo[:, :, 512:640], bank[1][:, :].rearrange("p (a n) -> p a n", n=P))
                rope(2)
                plain(hid_hi[:, 0, 0:Tq], hid_lo[:, 0, 0:Tq], bank[2][:, 0:Tq])
                chain_lo(2)
                head_norm(4)
                plain(hid_hi[:, 1, 0:Tq], hid_lo[:, 1, 0:Tq], bank[3][:, 0:Tq])
                lo_split(u + 5)
                rope(3)
                chain_lo(3)
                rope(4)
                chain_lo(4)
                for j in range(4, IN_UNITS):
                    beside = layer == 0 and j in MODS_BESIDE_IN
                    job = planned("w_in")[MODS_BESIDE_IN.index(j)] if beside else None
                    if job:
                        mod_sum(job, range(KT))
                    plain_of(j, 0)
                    plain_of(j, 1)
                    if job:
                        mod_out(job[0], 6 + job[1])
                    lo_split(u + j + 2)

                work = items(layer)
                i0 = ITEMS0[layer]
                b0 = blocks_before(layer)
                for i in range(len(work) + O_LAG + 3):
                    if 1 <= i <= len(work):
                        dve.wait_ge(exp_done, i0 + i)
                        dve.reciprocal(linv[:, i - 1:i], lsum[:, i - 1:i]).then_inc(linv_done, 1)
                    if i < len(work):
                        g, tt, j, half = work[i]
                        N = TOK if tt < 2 else TOK - LAT
                        dve.wait_ge(s_mm, i0 + i + 1)
                        S = bank[i % 3]
                        if not g and tt < 2:
                            dve.wait_ge(bias_done, layer + 1)
                            latents = S[:, 0:LAT].rearrange("p (a b) -> p a b", a=ROWS)
                            link(dve.scalar_tensor_tensor(out=latents, in0=bias[:, tt, 2 * j + half, :, ::-1],
                                                          scalar=1.0 / SCALE, in1=latents, op0=ALU.mult, op1=ALU.add))
                        dve.tensor_scalar(S[:, 0:N], S[:, 0:N], -SCALE, None, ALU.mult, ALU.min,
                                          accum_out=nmax[:, i:i + 1]).then_inc(nm_done, 1)
                    if T_LAG <= i < len(work) + T_LAG:
                        k = i - T_LAG
                        kk = 4 if work[k][1] < 2 else 2
                        dve.wait_ge(pthi_done, i0 + k + 1)
                        dve.tensor_tensor(pt_lo[k // 2 % 2][:, k % 2, 0:kk, :],
                                          bank[3 + k % 3][:, 0:kk * P].rearrange("p (a n) -> p a n", n=P),
                                          pt_hi[k // 2 % 2][:, k % 2, 0:kk, :].bitcast(F32), ALU.subtract).then_inc(ptlo_done, 1)
                    k = i - O_LAG - 1
                    if k >= BLOCK and k % BLOCK == 0:
                        b = k // BLOCK - 1
                        dve.wait_ge(ysq_done, b0 + b + 1)
                        if b >= 4:
                            dve.wait_ge(yss_mm, b0 + b - 3)
                        dve.tensor_reduce(scr[5][:, b % 4 * P:(b % 4 + 1) * P],
                                          scr[4][:, :].rearrange("p (a t) -> p t a", a=4),
                                          mybir.AxisListType.X, ALU.add).then_inc(ysum_done, 1)
                tts = Tq // P
                dve.wait_ge(yrms_done, layer + 1)
                groups = rms[:, 7 + 2 * layer:9 + 2 * layer, 0:tts]
                link(dve.reciprocal(groups, groups))
                for g in (1, 0):
                    dve.tensor_tensor(scr[g][:, 0:Tq].rearrange("p (a t) -> p a t", a=tts),
                                      ident.unsqueeze(1).broadcast_to([P, tts, P]),
                                      rms[:, 7 + 2 * layer + g, 0:tts].unsqueeze(2).broadcast_to([P, tts, P]),
                                      ALU.mult).then_inc(ydiag_done, 1)
                for n in range(KT + AHEAD):
                    if n < KT:
                        ct = Y_ORDER[n]
                        dve.wait_ge(yrstd_mm, 2 * layer + (1 if ct >= 4 else 2))
                        dve.tensor_tensor(yn[:, ct, 0:Tq], y[:, ct, 0:Tq], bank[ct // 4][:, 0:Tq],
                                          ALU.mult).then_inc(yn_done, 1)
                    if n >= AHEAD:
                        ct = Y_ORDER[n - AHEAD]
                        dve.wait_ge(y_hi_done, KT * layer + n - AHEAD + 1)
                        dve.scalar_tensor_tensor(out=hid_lo[:, ct, 0:Tq], in0=yn[:, ct, 0:Tq],
                                                 scalar=vec[:, layer, V_GO + ct:V_GO + ct + 1],
                                                 in1=hid_hi[:, ct, 0:Tq].bitcast(F32),
                                                 op0=ALU.mult, op1=ALU.subtract).then_inc(y_done, 1)
                prepare_gate(layer, 5, 1.0)
                uo = out_unit(layer)
                jobs = planned("w_out") if layer == 0 else []
                for j in range(OUT_UNITS):
                    for job in jobs[j:j + 1]:
                        mod_sum(job, range(KT))
                    update(uo + j, j, (4, 5) if j % 2 == 0 else (6, 7), Tq, 3 * layer + 2)
                    for job in (jobs[j - 1:j] if j > 0 else []) + (jobs[j:] if j == OUT_UNITS - 1 else []):
                        mod_out(job[0], job[1])

            dve.memset(ones[:, :], 1.0)
            dve.memset(eps[:, 0:1], EPS).then_inc(ready, 1)
            dve.memset(lsum[:, :], 1.0).then_inc(silu_done, BANKS_FREE)
            dve.memset(nmax[:, :], 0.0).then_inc(prod_done, BANKS_FREE)
            dve.wait_ge(prod_done, BANKS_FREE)
            dve.wait_ge(cs_done, 1)
            for m, s, _, _ in planned("first"):
                if by_vector(m):
                    mod_sum((m, s, 0, None), range(KT))
                if m == 1:
                    add_squares(0, range(KT))
                if m == 3:
                    dve.wait_ge(more_in, 32)
                    inverse(0)
                if m == 5:
                    lo_split(0)
            lo_split(1)
            dve.wait_ge(mod_mm, MODS_FIRST)
            first = 2 * MODS_FIRST
            dve.tensor_tensor(mod[:, 0:first, :], bank[6][:, 0:2 * first].rearrange("p (a c) -> p a c", c=2),
                              bm[:, 0:first].unsqueeze(2).broadcast_to([P, first, 2]), ALU.add).then_inc(mod_done, MODS_FIRST)
            prepare(0, V_N1, 0)
            norm(0, 0)
            for layer in range(DEPTH):
                ffn(layer, False)
                prepare(layer, V_NMIX, 3)
                norm(3 * layer + 1, 9 * layer + 3)
                mixer(layer)
                prepare(layer, V_N2, 6)
                norm(3 * layer + 2, 9 * layer + 6)
                ffn(layer, True)
                if layer < DEPTH - 1:
                    prepare(layer + 1, V_N1, 0)
                norm(3 * layer + 3, 9 * (layer + 1))

        @block.gpsimd
        def _(pool):
            def norm(n):
                T = norm_tok[n]
                for kt in POOL_KT:
                    pool.wait_ge(hf_done, hf_before(n) + (T // LAT) * kt)
                    pool.tensor_copy(h_hi[:, kt, 0:T], hf[:, kt, 0:T]).then_inc(hhi_pool, 1)

            def mask(layer):
                pool.wait_ge(bias_in, 16 * ROWS * ROWS * (layer + 1))
                masks = 0
                for lo, sign, base in ((WIN_W, -1, GRID_W - 1 + WIN_W // 2), (0, 1, WIN_W // 2 - GRID_W)):
                    for qt in range(2):
                        for p0 in (0, GRID_W):
                            v = bias[p0:p0 + GRID_W, qt].rearrange("p h r c -> p (h r) c")[:, :, lo:lo + GRID_W - WIN_W]
                            pool.affine_select(out=v, in_=v, compare_op=ALU.is_ge, fill=-1e30,
                                               base=base + sign * lo,
                                               pattern=[[0, HEADS * ROWS], [sign, GRID_W - WIN_W]],
                                               channel_multiplier=sign).then_inc(g_masked, 1)
                    masks += 4
                    pool.wait_ge(g_masked, 8 * layer + masks)
                pool.memset(flag[:, :], 0.0).then_inc(bias_done, 1)

            norm(0)
            for layer in range(DEPTH):
                norm(3 * layer + 1)
                mask(layer)
                norm(3 * layer + 2)
                if layer < DEPTH - 1:
                    norm(3 * layer + 3)

        @block.tensor
        def _(pe):
            def product(out, terms, waits=None):
                n, of = terms
                for kt in range(n):
                    if waits is not None:
                        pe.wait_ge(waits[0], waits[1] + kt + 1)
                    a_hi, a_lo, b_hi, b_lo = of(kt)
                    pe.matmul(out, a_hi, b_hi, start=kt == 0, stop=False)
                    pe.matmul(out, a_hi, b_lo, start=False, stop=False)
                    mm = pe.matmul(out, a_lo, b_hi, start=False, stop=kt == n - 1)
                return mm

            def weights(s, c0, width, rhs_hi, rhs_lo, T, n=KT):
                return n, lambda kt: (whi[s][:, kt, c0:c0 + width], wlo[s][:, kt, c0:c0 + width],
                                      rhs_hi[:, kt, 0:T], rhs_lo[:, kt, 0:T])

            def mod_total(m, s, b, i=0):
                col = 4 * m if m < MODS_FIRST else 0
                if m >= MODS_FIRST:
                    pe.wait_ge(mod_done, i + (m - 1))
                pe.wait_ge(mod_step, i * MSTEPS + mod_steps(m + 1))
                for t in range(2):
                    for c in range(2):
                        to = col + 2 * t + c
                        mm = pe.matmul(bank[b][:, to:to + 1], macc[s][:, c, t * P:(t + 1) * P], ones[:, 0:1],
                                       start=True, stop=True)
                mm.then_inc(mod_mm, 1)

            def mod_unit(m):
                pe.wait_ge(mfirst_in[m], 16)
                for t in range(2):
                    for kt in range(KT):
                        mm = pe.matmul(bank[6][:, 4 * m + 2 * t:4 * m + 2 * t + 2], mfirst[m][:, kt, t * P:(t + 1) * P],
                                       cs[:, kt, :], start=kt == 0, stop=kt == KT - 1)
                mm.then_inc(mod_mm, 1)

            def stats(n):
                pe.wait_ge(acc_done, (KT - 1) * (n + 1))
                for a in range(norm_tok[n] // P):
                    mm = pe.matmul(bank[4][:, a:a + 1], scr[2][:, a * P:(a + 1) * P], ones[:, 0:1],
                                   start=True, stop=True)
                mm.then_inc(ssq_mm, 1)

            def spread(n):
                T = norm_tok[n]
                pe.wait_ge(diag_done, n + 1)
                pe.matmul(bank[5][:, 0:T], ones[:, :], scr[3][:, 0:T], start=True, stop=True).then_inc(rstd_mm, 1)

            def first_unit(banks, s, a_hi, a_lo, order, done, before, T):
                for n, kt in enumerate(order):
                    pe.wait_ge(done, before + n + 1)
                    for t in range(2):
                        out = bank[banks[t]][:, 0:T]
                        hi, lo = whi[s][:, kt, t * P:(t + 1) * P], wlo[s][:, kt, t * P:(t + 1) * P]
                        pe.matmul(out, hi, a_hi[:, kt, 0:T], start=n == 0, stop=False)
                        pe.matmul(out, hi, a_lo[:, kt, 0:T], start=False, stop=False)
                        mm = pe.matmul(out, lo, a_hi[:, kt, 0:T], start=False, stop=n == KT - 1)
                        if n == KT - 1:
                            mm.then_inc(half_mm if t == 0 else unit_mm[s], 1)

            def ffn(layer, second):
                T = tokens(layer, 2 * second)
                n_norm = 3 * layer + 2 * second
                u = ffn_unit(layer, second)
                tile = HTILES * (2 * layer + second)
                xb = x_before(layer, 2 * second)
                for chunk, n in enumerate(CHUNKS):
                    job = paired(("pairs", layer, second, chunk))
                    jobs = planned("w2", layer, second, chunk)

                    def pair(i, first):
                        for j in range(2):
                            s = (u + j) % 2
                            pe.wait_ge(split[s], i + ((u + j) // 2 + 1))
                            if j == 1 and xb > 0:
                                pe.wait_ge(x_done, xb)
                            if j == 0 and first:
                                pe.wait_ge(prod_done, tile + 2)
                                first_unit((0, 1), s, h_hi, h_lo, H_ORDER, h_done, KT * n_norm, T)
                                continue
                            for t in range(2):
                                pe.wait_ge((prod_done, silu_done)[j], i * 2 + (tile + t + 1))
                                mm = product(bank[2 * j + t][:, 0:T], weights(s, t * P, P, h_hi, h_lo, T))
                                mm.then_inc(half_mm if t == 0 else unit_mm[s], 1)
                                if j == 1 and t == 0 and job:
                                    mod_total(job[0], job[1], 6 + job[1], i)

                    if chunk == 0:
                        pair(0, True)
                    with pe.Fori(1 if chunk == 0 else 0, n) as i:
                        pair(i, False)
                    u += 2 * n
                    for j in range(W2_UNITS):
                        s = u % 2
                        pe.wait_ge(split[s], u // 2 + 1)
                        b = 4 if j % 2 == 0 else 2
                        for t in range(2):
                            if j >= 2:
                                pe.wait_ge(x_done, xb + 2 * (j - 2) + t + 1)
                            elif j == 0 and xb > 0:
                                pe.wait_ge(x_done, xb)
                            mm = product(bank[b + t][:, 0:T], weights(s, t * P, P, hid_hi, hid_lo, T, 2 * n),
                                         (hid_done, tile) if j == 0 and t == 0 else None)
                            mm.then_inc(half_mm if t == 0 else unit_mm[s], 1)
                            due = jobs[j - 1:j] if t == 0 and j > 0 else jobs[j:] if j == W2_UNITS - 1 else []
                            for mod_job in due:
                                mod_total(mod_job[0], mod_job[1], 6 + mod_job[1])
                        u += 1
                    tile += 2 * n
                    xb += KT

            def mixer(layer):
                u0 = in_unit(layer)
                Tq = tokens(layer, 2)
                cb, pb = CHAINS * layer, PLAIN * layer
                xb = x_before(layer, 1)

                def tile_of(j, t):
                    u = u0 + j
                    s = u % 2
                    if t == 0:
                        pe.wait_ge(split[s], u // 2 + 1)
                    b = 2 * (j % 2) + t
                    if j == 2 and t == 0:
                        pe.wait_ge(qsq, cb + 1)
                    elif j == 2:
                        pe.wait_ge(qsq, cb + 2)
                    elif j == 3:
                        pe.wait_ge(qsq, cb + 3 + t)
                    elif j == 4 and t == 0:
                        pe.wait_ge(qsq, cb + 5)
                    elif j == 4:
                        pe.wait_ge(pj_done, pb + 1)
                    elif j >= 5:
                        pe.wait_ge(pj_done, pb + 2 * (j - 5) + t + 2)
                    if j >= 7 or (j, t) == (2, 1):
                        c0, width, tts = (P, P, range(4)) if j == 2 else (0, UW, range(2 * t, 2 * t + 2))
                        for a, tt in enumerate(tts):
                            tk = slice(tt * P, (tt + 1) * P)
                            mm = product(bank[b][:, a * width:(a + 1) * width],
                                         (KT, lambda kt: (h_hi[:, kt, tk], h_lo[:, kt, tk],
                                                          whi[s][:, kt, c0:c0 + width], wlo[s][:, kt, c0:c0 + width])))
                    else:
                        T = Tq if j < 5 and j != 2 else TOK
                        mm = product(bank[b][:, 0:T], weights(s, t * P, P, h_hi, h_lo, T))
                    mm.then_inc(half_mm if t == 0 else unit_mm[s], 1)

                def head_sums(n):
                    T = TOK if n == 4 else Tq
                    pe.wait_ge(qsq, cb + n + 1)
                    if n >= 2:
                        pe.wait_ge(qsd, cb + n - 1)
                    pe.matmul(bank[4 + n % 2][:, 0:T], blk, scr[(2, 3, 5)[n % 3]][:, 0:T], start=True,
                              stop=True).then_inc(qss_mm, 1)

                def rotate(n):
                    pe.wait_ge(qn_done, cb + n + 1)
                    if n >= 2:
                        pe.wait_ge(rope_done, cb + n - 1)
                    pe.matmul(bank[6 + n % 2][:, 0:LAT], rot, scr[(0, 1, 4)[n % 3]][:, 0:LAT], start=True,
                              stop=True).then_inc(rot_mm, 1)

                pe.wait_ge(split[u0 % 2], u0 // 2 + 1)
                pe.wait_ge(x_done, xb)
                first_unit((0, 1), u0 % 2, h_hi, h_lo, H_ORDER, h_done, KT * (3 * layer + 1), Tq)
                tile_of(1, 0)
                head_sums(0)
                head_sums(1)
                tile_of(1, 1)
                tile_of(2, 0)
                rotate(0)
                rotate(1)
                head_sums(2)
                tile_of(2, 1)
                head_sums(3)
                tile_of(3, 0)
                rotate(2)
                head_sums(4)
                tile_of(3, 1)
                rotate(3)
                tile_of(4, 0)
                rotate(4)
                for j in range(4, IN_UNITS):
                    if j > 4:
                        tile_of(j, 0)
                    tile_of(j, 1)
                    if layer == 0 and j in MODS_BESIDE_IN:
                        m, s, _, _ = planned("w_in")[MODS_BESIDE_IN.index(j)]
                        mod_total(m, s, 6 + s)

                work = items(layer)
                i0 = ITEMS0[layer]
                b0 = blocks_before(layer)
                pe.wait_ge(qk_done, cb + CHAINS)
                pe.wait_ge(pj_done, pb + PLAIN)
                for i in range(len(work) + O_LAG + 3):
                    if i < len(work):
                        g, tt, j, half = work[i]
                        kt = 4 if g else j
                        ks = slice(0, TOK) if tt < 2 else slice(LAT, TOK)
                        N = ks.stop - ks.start
                        pp = slice(half * HD, (half + 1) * HD)
                        tk = slice(tt * P, (tt + 1) * P)
                        if i >= 3:
                            pe.wait_ge(exp_done, i0 + i - 2)
                        product(bank[i % 3][:, 0:N],
                                (1, lambda _: (hid_hi[pp, 4 * g + j, tk], hid_lo[pp, 4 * g + j, tk],
                                               k_hi[pp, kt, ks], k_lo[pp, kt, ks]))).then_inc(s_mm, 1)
                    if T_LAG <= i < len(work) + T_LAG:
                        k = i - T_LAG
                        kk = 4 if work[k][1] < 2 else 2
                        pe.wait_ge(pdiag_done, i0 + k + 1)
                        if k >= 3:
                            pe.wait_ge(ptlo_done, i0 + k - 2)
                        for a in range(kk):
                            mm = pe.matmul(bank[3 + k % 3][:, a * P:(a + 1) * P], scr[k % 3][:, a * P:(a + 1) * P],
                                           scr[3][:, k % 3 * P:(k % 3 + 1) * P], start=True, stop=True)
                        mm.then_inc(t_mm, 1)
                    k = i - O_LAG
                    if 0 <= k < len(work) and k % 2 == 1:
                        g, tt, j, _ = work[k]
                        kk = 4 if tt < 2 else 2
                        c = HEADS * HD if g else P * j
                        b = k // 2 % 2
                        pe.wait_ge(ptlo_done, i0 + k + 1)
                        if k >= 4:
                            pe.wait_ge(y_out_done, i0 + k - 3)
                        product(bank[6 + b][:, 0:2 * P].rearrange("p (h t) -> p h t", h=2),
                                (kk, lambda a: (v_hi[:, 4 - kk + a, c:c + P], v_lo[:, 4 - kk + a, c:c + P],
                                                pt_hi[b][:, :, a, :], pt_lo[b][:, :, a, :]))).then_inc(o_mm, 1)
                    k = i - O_LAG - 2
                    if k >= BLOCK and k % BLOCK == 0:
                        b = k // BLOCK - 1
                        g, tt = work[k - 1][:2]
                        pe.wait_ge(ysum_done, b0 + b + 1)
                        pe.matmul(bank[7][:, 256 + 4 * g + tt:257 + 4 * g + tt], scr[5][:, b % 4 * P:(b % 4 + 1) * P],
                                  ones[:, 0:1], start=True, stop=True).then_inc(yss_mm, 1)
                for n, g in enumerate((1, 0)):
                    pe.wait_ge(ydiag_done, 2 * layer + n + 1)
                    pe.matmul(bank[g][:, 0:Tq], ones[:, :], scr[g][:, 0:Tq], start=True,
                              stop=True).then_inc(yrstd_mm, 1)
                jobs = planned("w_out") if layer == 0 else []
                for j in range(OUT_UNITS):
                    u = out_unit(layer) + j
                    s = u % 2
                    pe.wait_ge(split[s], u // 2 + 1)
                    b = 4 if j % 2 == 0 else 6
                    if j == 0:
                        first_unit((4, 5), s, hid_hi, hid_lo, Y_ORDER, y_done, KT * layer, Tq)
                    for t in range(2):
                        if j >= 2:
                            pe.wait_ge(x_done, xb + 2 * (j - 2) + t + 1)
                        if j == 0:
                            continue
                        mm = product(bank[b + t][:, 0:Tq], weights(s, t * P, P, hid_hi, hid_lo, Tq))
                        mm.then_inc(half_mm if t == 0 else unit_mm[s], 1)
                        due = jobs[j - 1:j] if t == 0 and j > 0 else jobs[j:] if j == OUT_UNITS - 1 else []
                        for m, slot, _, _ in due:
                            mod_total(m, slot, slot)

            pe.wait_ge(ready, 1)
            pe.wait_ge(cs_done, 1)
            for m in FIRST_ORDER:
                if by_vector(m):
                    mod_total(m, m // 2 % 2, 6)
                else:
                    mod_unit(m)
                if m == 1:
                    stats(0)
                if m == 3:
                    spread(0)
            for layer in range(DEPTH):
                ffn(layer, False)
                stats(3 * layer + 1)
                spread(3 * layer + 1)
                mixer(layer)
                stats(3 * layer + 2)
                spread(3 * layer + 2)
                ffn(layer, True)
                stats(3 * layer + 3)
                spread(3 * layer + 3)


def _constants():
    c = np.zeros((P, C_COLS), np.float32)
    r = np.arange(P)
    c[:, C_ID:C_ID + P] = np.eye(P, dtype=np.float32)
    c[:, C_BLK:C_BLK + P] = (r[:, None] // HD == r[None, :] // HD).astype(np.float32)
    for m in range(P):
        first = m % 32 < 16
        c[m + 16 if first else m - 16, C_ROT + m] = -1.0 if first else 1.0
    t = np.arange(LAT)
    step = -np.arange(0, HD // 2, 2, dtype=np.float32) / np.float32(HD // 2)
    inv = (np.float32(ROPE_THETA) ** step).astype(np.float32)
    for m in range(P):
        d = m % HD
        pos = (t // GRID_W if d < HD // 2 else t % GRID_W).astype(np.float32)
        ang = pos * inv[d % 16]
        c[m, C_COS:C_COS + LAT] = np.cos(ang)
        c[m, C_SIN:C_SIN + LAT] = np.sin(ang)
    return c


def kernel(x, c, ctx, c_ctx, w_mod, b_mod, norm_ffn1, ffn1_w13, ffn1_w2, norm_mix, w_in, na_rpb,
           gqa_q_norm, gqa_k_norm, out_norm_a, out_norm_b, w_out, norm_ffn2, ffn2_w13, ffn2_w2, norm_f):
    import concourse.bacc as bacc
    from concourse.bass_utils import run_bass_kernel_spmd

    def columns(v):
        return np.asarray(v).reshape(-1, P).T

    def paired_heads(v):
        return np.asarray(v).reshape(2, 4, HD).transpose(1, 0, 2).reshape(-1)

    per_layer = []
    for i in range(DEPTH):
        cond = np.stack([columns(c), columns(c_ctx)], axis=2).reshape(P, 2 * KT)
        head = [np.concatenate([g[i], g[i]]).reshape(P, 1) for g in (np.asarray(gqa_q_norm), np.asarray(gqa_k_norm))]
        per_layer.append(np.concatenate(
            [columns(norm_ffn1[i]), columns(norm_mix[i]), columns(norm_ffn2[i]), columns(out_norm_a[i]),
             columns(paired_heads(out_norm_b[i])), *head, columns(norm_f), cond], axis=1))
    arrays = {
        "xT": np.asarray(x)[0].T, "ctxT": np.asarray(ctx)[0].T,
        "vecs": np.stack(per_layer, axis=1), "bmod": columns(b_mod), "consts": _constants(),
        "w_mod": w_mod, "ffn1_w13": ffn1_w13, "ffn1_w2": ffn1_w2, "w_in": w_in, "rpb": np.asarray(na_rpb)[..., ::-1],
        "w_out": w_out, "ffn2_w13": ffn2_w13, "ffn2_w2": ffn2_w2,
    }
    arrays = {n: np.ascontiguousarray(a) for n, a in arrays.items()}
    nc = bacc.Bacc("TRN2", target_bir_lowering=False, num_devices=1)
    args = [nc.dram_tensor(n, a.shape, mybir.dt.from_np(a.dtype), kind="ExternalInput").ap() for n, a in arrays.items()]
    out = nc.dram_tensor("outT", (D, LAT), F32, kind="ExternalOutput").ap()
    build(nc, *args, out)
    r = run_bass_kernel_spmd(nc, [arrays], core_ids=[0])
    return np.ascontiguousarray(r.results[0]["outT"].T).reshape(1, LAT, D)
```
